# Optimizing a Trainium2 kernel written in Bass

```python
import jax, jax.numpy as jnp
from jax import lax
import numpy as np

D_MODEL = 1024
BATCH = 1
SEQ = 1024
DEPTH = 1

MIX_WIDTH = D_MODEL
POOL_WIDTH = MIX_WIDTH // 2
POOL_WINDOWS = (2, 4, 8, 16)
N_POOL_GROUPS = len(POOL_WINDOWS)
POOL_GROUP_DIM = POOL_WIDTH // N_POOL_GROUPS
ATTN_WIDTH = MIX_WIDTH - POOL_WIDTH
HEAD_DIM = 64
N_Q_HEADS = ATTN_WIDTH // HEAD_DIM
N_KV_HEADS = 2
GQA_GROUP = N_Q_HEADS // N_KV_HEADS
WINDOW = 128
BLOCK = 128
N_BUCKETS = 32
MAX_EXACT = N_BUCKETS // 2
MAX_DISTANCE = 128
IN_WIDTH = POOL_WIDTH + N_Q_HEADS * HEAD_DIM + 2 * N_KV_HEADS * HEAD_DIM
D_FF = -(-(8 * D_MODEL) // (3 * 256)) * 256
EPS = 1e-6
NEG_INF = -1e30

kernel_name = "hybrid_pool_swa_sink_t5bias_block"

def rmsnorm(x, g):
    xf = x.astype(jnp.float32)
    xf = xf * lax.rsqrt(jnp.mean(xf * xf, axis=-1, keepdims=True) + EPS)
    return xf.astype(x.dtype) * g

def multiscale_pool(u, w_pool, pool_scale):
    b, s, _ = u.shape
    ug = u.reshape(b, s, N_POOL_GROUPS, POOL_GROUP_DIM)
    csum = jnp.cumsum(ug.astype(jnp.float32), axis=1)
    pos = jnp.arange(1, s + 1, dtype=jnp.float32)
    pooled = []
    for g, w in enumerate(POOL_WINDOWS):
        c = csum[:, :, g]
        lagged = jnp.pad(c, ((0, 0), (w, 0), (0, 0)))[:, :s]
        count = jnp.minimum(pos, float(w))[None, :, None]
        pooled.append((c - lagged) / count)
    pooled = jnp.stack(pooled, axis=2).astype(u.dtype) - ug
    mixed = jnp.einsum('bsgc,gcd->bsgd', pooled, w_pool)
    return mixed.reshape(b, s, POOL_WIDTH) * pool_scale

def relative_bias_band(rel_bias):
    qi = jnp.arange(BLOCK)[:, None]
    kj = jnp.arange(2 * BLOCK)[None, :]
    dist = qi + BLOCK - kj
    n = jnp.maximum(dist, 0)
    nf = jnp.maximum(n, 1).astype(jnp.float32)
    large = MAX_EXACT + (jnp.log(nf / MAX_EXACT) / np.float32(np.log(MAX_DISTANCE / MAX_EXACT))
                         * (N_BUCKETS - MAX_EXACT)).astype(jnp.int32)
    large = jnp.minimum(large, N_BUCKETS - 1)
    bucket = jnp.where(n < MAX_EXACT, n, large)
    bias = rel_bias.astype(jnp.float32)[bucket]
    bias = jnp.transpose(bias, (2, 0, 1)).reshape(N_KV_HEADS, GQA_GROUP, BLOCK, 2 * BLOCK)
    in_window = (dist >= 0) & (dist < WINDOW)
    return bias, in_window

def sliding_window_attention(q, k, v, rel_bias, sinks):
    b, s = q.shape[:2]
    nb = s // BLOCK
    qb = q.reshape(b, nb, BLOCK, N_KV_HEADS, GQA_GROUP, HEAD_DIM)

    def band(t):
        prev = jnp.pad(t, ((0, 0), (BLOCK, 0), (0, 0), (0, 0)))[:, :s]
        prev = prev.reshape(b, nb, BLOCK, N_KV_HEADS, HEAD_DIM)
        cur = t.reshape(b, nb, BLOCK, N_KV_HEADS, HEAD_DIM)
        return jnp.concatenate([prev, cur], axis=2)

    kb, vb = band(k), band(v)
    bias, in_window = relative_bias_band(rel_bias)
    key_exists = (jnp.arange(nb)[:, None] > 0) | (jnp.arange(2 * BLOCK)[None, :] >= BLOCK)
    mask = in_window[None] & key_exists[:, None, :]
    scale = 1.0 / np.sqrt(HEAD_DIM).astype(np.float32)
    logits = jnp.einsum('bnqhgd,bnkhd->bnhgqk', qb, kb).astype(jnp.float32) * scale
    logits = logits + bias[None, None]
    logits = jnp.where(mask[None, :, None, None], logits, NEG_INF)
    sink = sinks.astype(jnp.float32).reshape(N_KV_HEADS, GQA_GROUP)[None, None, :, :, None, None]
    m = jnp.maximum(jnp.max(logits, axis=-1, keepdims=True), sink)
    p = jnp.exp(logits - m)
    denom = jnp.sum(p, axis=-1, keepdims=True) + jnp.exp(sink - m)
    probs = (p / denom).astype(v.dtype)
    out = jnp.einsum('bnhgqk,bnkhd->bnqhgd', probs, vb)
    return out.reshape(b, s, ATTN_WIDTH)

def setup_inputs(seed: int = 0) -> dict:
    key = jax.random.key(seed)
    ks = jax.random.split(key, 16)
    f32 = jnp.float32

    def w(k, shape, fan_in):
        return jax.random.normal(k, shape, f32) * (fan_in ** -0.5)

    def gain(k, shape):
        return 1.0 + 0.05 * jax.random.normal(k, shape, f32)

    return {
        "x": jax.random.normal(ks[0], (BATCH, SEQ, D_MODEL), f32),
        "g_pre_mix": gain(ks[1], (DEPTH, D_MODEL)),
        "w_in": w(ks[2], (DEPTH, D_MODEL, IN_WIDTH), D_MODEL),
        "w_pool": w(ks[3], (DEPTH, N_POOL_GROUPS, POOL_GROUP_DIM, POOL_GROUP_DIM), POOL_GROUP_DIM),
        "pool_scale": 1.0 + 0.1 * jax.random.normal(ks[4], (DEPTH, POOL_WIDTH), f32),
        "rel_bias": 0.5 * jax.random.normal(ks[5], (N_BUCKETS, N_Q_HEADS), f32),
        "sinks": 0.5 * jax.random.normal(ks[6], (DEPTH, N_Q_HEADS), f32),
        "w_out": w(ks[7], (DEPTH, MIX_WIDTH, D_MODEL), MIX_WIDTH),
        "g_post_mix": gain(ks[8], (DEPTH, D_MODEL)),
        "g_pre_ffn": gain(ks[9], (DEPTH, D_MODEL)),
        "w_gate": w(ks[10], (DEPTH, D_MODEL, D_FF), D_MODEL),
        "w_up": w(ks[11], (DEPTH, D_MODEL, D_FF), D_MODEL),
        "w_down": w(ks[12], (DEPTH, D_FF, D_MODEL), D_FF),
        "g_post_ffn": gain(ks[13], (DEPTH, D_MODEL)),
    }

def reference(x, g_pre_mix, w_in, w_pool, pool_scale, rel_bias, sinks, w_out,
              g_post_mix, g_pre_ffn, w_gate, w_up, w_down, g_post_ffn):
    b, s, _ = x.shape
    q_end = POOL_WIDTH + N_Q_HEADS * HEAD_DIM
    k_end = q_end + N_KV_HEADS * HEAD_DIM
    for l in range(DEPTH):
        h = rmsnorm(x, g_pre_mix[l])
        proj = h @ w_in[l]
        u = proj[..., :POOL_WIDTH]
        q = proj[..., POOL_WIDTH:q_end].reshape(b, s, N_Q_HEADS, HEAD_DIM)
        k = proj[..., q_end:k_end].reshape(b, s, N_KV_HEADS, HEAD_DIM)
        v = proj[..., k_end:].reshape(b, s, N_KV_HEADS, HEAD_DIM)
        pool_out = multiscale_pool(u, w_pool[l], pool_scale[l])
        attn_out = sliding_window_attention(q, k, v, rel_bias, sinks[l])
        mix = jnp.concatenate([pool_out, attn_out], axis=-1) @ w_out[l]
        x = x + rmsnorm(mix, g_post_mix[l])
        h = rmsnorm(x, g_pre_ffn[l])
        f = (jax.nn.silu(h @ w_gate[l]) * (h @ w_up[l])) @ w_down[l]
        x = x + rmsnorm(f, g_post_ffn[l])
    return x


_drawn_inputs = setup_inputs


def setup_inputs(seed=0):
    import zlib

    import numpy as np

    out = dict(_drawn_inputs(seed))
    spreads = {}
    factors = {'sinks': 8.0}
    for name, (base, spread) in spreads.items():
        noise = np.random.default_rng([zlib.crc32(name.encode()), seed]).standard_normal(out[name].shape)
        drawn = base * np.exp(spread * noise) if base else spread * noise
        out[name] = __import__('jax').numpy.asarray(drawn.astype(out[name].dtype))
    for name, factor in factors.items():
        out[name] = (out[name] * factor).astype(out[name].dtype)
    return out
```

```python
from contextlib import ExitStack

import numpy as np

import concourse.bass as bass
from concourse import mybir

F32 = mybir.dt.float32
F32R = mybir.dt.float32r
ALU = mybir.AluOpType
ACT = mybir.ActivationFunctionType

P = 128
SEQ = 1024
D = 1024
HALVES = 2
T = SEQ // HALVES
KD = D // P
HEAD_DIM = 64
N_HEADS = 8
N_KV = 2
BLOCK = 128
BLOCKS = SEQ // BLOCK
WINDOWS = (2, 4, 8, 16)
HIST = 16
N_BUCKETS = 32
D_FF = 2816
FF_TILES = D_FF // P
FF_PER_GROUP = 2
GROUPS = FF_TILES // FF_PER_GROUP
EPS = 1e-6
MASKED = -1e30
SCALE = HEAD_DIM ** -0.5
BAND = 384

G_PRE_MIX, G_POST_MIX, G_PRE_FFN, G_POST_FFN, POOL_SCALE, SINKS = 0, 8, 16, 24, 32, 36
N_SMALL = 44
IDENT, FLIP, ONES, INV_COUNT = 0, 128, 256, 384
N_CONST = 384 + HIST

RING = 3
RAW = 2
UNITS = 16
HI, LO = 0, 1


def unit_place(u):
    half = u // 8
    return half, (u // 4) % 2, 4 * half + u % 4


def key_blocks(u):
    return (1,) if unit_place(u)[2] == 0 else (0, 1)


def make_schedule():
    pre = [("proj", 0, "k"), ("proj", 0, "v"), ("norm", "x", 0), ("bias",), ("proj", 0, "q0"), ("vtr", 0),
           ("proj", 0, "q1"), ("proj", 0, "u0"), ("proj", 0, "u1"), ("norm", "x", 1), ("proj", 0, "u2"),
           ("proj", 0, "u3"), ("proj", 0, "q2"), ("proj", 0, "q3")]
    fill = {s: [("proj", 1, n)] for s, n in enumerate(("u0", "u1", "u2", "u3", "q0", "q1", "k", "v", "q2", "q3"))}
    for t in range(KD):
        fill[10 + t] = [("out", 0, t)]
    for g in range(4):
        fill[1 + g].append(("mix", 0, g))
        fill[11 + g].append(("mix", 1, g))
    pe = list(pre)
    for s in range(UNITS + 2):
        if s >= 2:
            pe.append(("values", s - 2))
        pe += fill[s]
        if 1 <= s <= UNITS:
            pe.append(("transpose", s - 1))
        if s == 7:
            pe.append(("vtr", 1))
        if s < UNITS:
            pe.append(("scores", s))
    pe += [("out", 1, 0), ("norm", "mix", 0)] + [("out", 1, t) for t in range(1, KD)]
    weights = [i for i in pe if i[0] in ("proj", "mix", "out")]

    tl = [("weights", 0), ("xsplit", 0), ("weights", 1), ("xsquares", 0), ("weights", 2), ("evac", ("norm", "x", 0)),
          ("evac", ("proj", 0, "k"))]

    def evac(item):
        if item[0] in ("proj", "mix", "out"):
            tl.append(("weights", weights.index(item) + 2))
        tl.append(("evac", item))

    evac(("proj", 0, "v"))
    tl += [("evac", ("bias",)), ("weights", 4), ("evac", ("vtr", 0)), ("evac", ("proj", 0, "q0")), ("bias_read",)]
    evac(("proj", 0, "q1"))
    tl += [("xsplit", 1), ("xsquares", 1)]
    evac(("proj", 0, "u0"))
    tl.append(("pool", 0, 0))
    evac(("proj", 0, "u1"))
    tl += [("evac", ("norm", "x", 1)), ("pool", 0, 1)]
    evac(("proj", 0, "u2"))
    tl.append(("pool", 0, 2))
    evac(("proj", 0, "u3"))
    tl.append(("pool", 0, 3))
    evac(("proj", 0, "q2"))
    evac(("proj", 0, "q3"))
    tl += [("pool_split", 0, g) for g in range(4)]
    for s in range(UNITS + 2):
        if 1 <= s <= UNITS:
            tl.append(("logits", s - 1))
        if s >= 2:
            tl.append(("heads_out", s - 2))
        if 1 <= s <= UNITS:
            tl.append(("exp", s - 1))
        tl += [("weights", weights.index(i) + 2) for i in fill[s]]
        if 1 <= s <= UNITS:
            tl.append(("normalise", s - 1))
        if 1 <= s <= 4:
            if s > 0:
                tl.append(("pool", 1, s - 1))
        for i in fill[s]:
            tl.append(("evac", i))
            if i[0] == "out":
                tl.append(("square", "mix", 0, i[2]))
        if 1 <= s <= UNITS:
            tl.append(("probs_split", s - 1))
        if s == 7:
            tl.append(("evac", ("vtr", 1)))
        if s == 10:
            tl += [("pool_split", 1, g) for g in range(4)]
    tl += [("x_load", 0, 0), ("x_load", 0, 1)]
    evac(("out", 1, 0))
    tl += [("evac", ("norm", "mix", 0)), ("square", "mix", 1, 0)]
    for t in range(KD):
        tl.append(("residual", 0, t))
        if t + 1 < KD:
            evac(("out", 1, t + 1))
            tl.append(("square", "mix", 1, t + 1))
    tl += [("weights", len(weights) + 2), ("weights", len(weights) + 3)]
    return pre, pe, weights, tl


PRE, PE_ORDER, WEIGHTS, TIMELINE = make_schedule()
N_RING = len(WEIGHTS)
assert N_RING % RAW == 0
NORMS_FIRST = [("norm", "x1", 0), ("norm", "mix", 1), ("norm", "x1", 1)]
NORMS_LAST = [("norm", "f", 0), ("norm", "f", 1)]
ITEMS = [i for i in PE_ORDER if i[0] in ("proj", "norm", "bias", "vtr", "mix", "out")] + NORMS_FIRST + NORMS_LAST
EVACS = [e[1] for e in TIMELINE if e[0] == "evac"] + NORMS_FIRST + NORMS_LAST
FULL = {i: n + 1 for n, i in enumerate(ITEMS)}
EVAC = {i: n + 1 for n, i in enumerate(EVACS)}
assert set(ITEMS) == set(EVACS) and len(ITEMS) == len(EVACS)


def make_banks():
    bank, before, last = {}, {}, {}
    n = 0
    for item in ITEMS:
        if item in PRE:
            b = (6, 7, 0, 1, 2, 3)[n % 6]
            n += 1
        elif item in NORMS_LAST:
            b = item[2]
            last.pop(b, None)
        else:
            b = 6 + n % 2
            n += 1
        bank[item] = b
        before[item] = last.get(b)
        last[b] = item
        if item == PRE[-1]:
            pre_last = dict(last)
    return bank, before, pre_last


BANK, BANK_BEFORE, PRE_LAST = make_banks()

SPLITS = {}
for _e in TIMELINE:
    if _e[0] == "evac" and _e[1][0] in ("vtr", "mix"):
        SPLITS[_e[1]] = len(SPLITS) + 1
    elif _e[0] == "evac" and _e[1][0] == "proj" and _e[1][2][0] in "qk":
        SPLITS[_e[1]] = len(SPLITS) + 1
    elif _e[0] == "pool_split":
        SPLITS[_e] = len(SPLITS) + 1

SQUARES = []
for _e in TIMELINE:
    if _e[0] == "xsquares":
        SQUARES += [("x", _e[1], k) for k in range(KD)]
    elif _e[0] == "square":
        SQUARES.append((_e[1], _e[2], _e[3]))
    elif _e[0] == "residual":
        SQUARES.append(("x1", _e[1], _e[2]))
SQUARES += [("x1", 1, t) for t in range(KD)]
SQUARES += [("f", h, t) for h in range(HALVES) for t in range(KD)]
SQUARE_NO = {s: n + 1 for n, s in enumerate(SQUARES)}
ADD_NO, _n = {}, 0
for _s in SQUARES:
    _n += _s[2] > 0
    ADD_NO[_s] = _n

PT_COUNT = [sum(len(key_blocks(v)) for v in range(u + 1)) for u in range(UNITS)]
WINDOW_STEPS = {}
_n = 0
for _h in range(HALVES):
    for _g in range(4):
        _n += _g + 1
        WINDOW_STEPS[(_h, _g)] = _n


def hybrid_layer(nc, x_t, small, consts, rel, onehot, w_in_t, w_pool, w_out_t, w_gate_t, w_up_t, w_down, out_t):
    with ExitStack() as ctx:
        def sb(name, shape, dt=F32):
            return ctx.enter_context(nc.sbuf_tensor(name, shape, dt))

        def sem(name):
            return ctx.enter_context(nc.semaphore(name))

        band_rows = nc.dram_tensor("band_rows", [N_HEADS, BAND], F32, kind="Internal").ap()
        x1_spill = nc.dram_tensor("x1_spill", [HALVES, P, KD, T], F32, kind="Internal").ap()

        mov = sb("mov", [P, 2, HALVES, KD, T], F32R)
        slots = sb("slots", [P, 4, 2, 1024], F32R)
        probs_t = slots[:, 3, :, :]
        qd = sb("qd", [P, 4096], F32R)
        q = qd[:, :].rearrange("p (j s t) -> p j s t", j=4, s=2)
        wd = qd[:, :].rearrange("p (c s n) -> p c s n", c=2, s=2)
        kvb = sb("kvb", [P, 4096 + 2 * BLOCKS * 192], F32R)
        kk = kvb[:, 0:4096].rearrange("p (s v t) -> p s v t", s=2, v=2)
        vv = kvb[:, 4096:4096 + 2 * BLOCKS * 192].rearrange("p (s b d) -> p s b d", s=2, b=BLOCKS)
        hid = kvb[:, 0:4096].rearrange("p (c s t) -> p c s t", c=2, s=2)

        big = sb("big", [P, HALVES, KD, T])
        area = big[:, 1, :, :].rearrange("p k t -> p (k t)")
        u_buf = area[:, 0:HIST + T]
        win = [area[:, (1 + i) * (HIST + T):(2 + i) * (HIST + T)] for i in range(2)]
        pooled = area[:, 3 * (HIST + T):3 * (HIST + T) + 4 * T].rearrange("p (g t) -> p g t", g=4)
        tails = area[:, 3 * (HIST + T) + 4 * T:3 * (HIST + T) + 4 * T + 4 * HIST].rearrange("p (g t) -> p g t", g=4)
        raw = sb("raw", [P, RAW, 1024])
        bias8 = sb("bias8", [P, N_HEADS * 256])
        late = bias8[:, :].rearrange("p (s t) -> p s t", s=4)
        lbuf = sb("lbuf", [P, 2, 1024])
        lq = lbuf[:, :, :].rearrange("p b (s t) -> p (b s) t", s=2)
        tmp = sb("tmp", [P, T])
        sum_mix = sb("sum_mix", [P, T])
        rms = sb("rms", [P, HALVES, T])
        sm = sb("sm", [P, N_SMALL])
        cst = sb("cst", [P, N_CONST])
        stat = sb("stat", [P, 2, 7, 4])
        fix = sb("fix", [P, HIST])
        rel_sb = sb("rel_sb", [N_BUCKETS + 1, N_HEADS])

        band_sb = bias8[0:N_HEADS, 0:BAND]
        ident, flip, ones = cst[:, IDENT:IDENT + P], cst[:, FLIP:FLIP + P], cst[:, ONES:ONES + P]

        ps = ctx.enter_context(nc.psum_tensor("ps", [P, 8, 512], F32))

        def scores_of(u, jj):
            return ps[:, 2 * (u % 2) + jj, :].rearrange("p (v k) -> p v k", v=2)

        def square_at(s):
            what, half, k = s
            if k == 0:
                return sum_at(what, half)
            if what == "x":
                return lq[:, k % 2, :]
            return late[:, 2, :] if what == "x1" else tmp[:, :]

        def sum_at(what, half):
            if what == "x":
                return lq[:, 2 + half, :]
            return late[:, 3, :] if what == "x1" else sum_mix[:, :]

        small_in = sem("small_in")
        onehot_in = sem("onehot_in")
        x_in = [sem(f"x_in{i}") for i in range(2 * HALVES)]
        raw_in = [sem(f"raw_in{i}") for i in range(RAW)]
        x_again = [sem(f"x_again{i}") for i in range(2)]
        spilled = [sem(f"spilled{h}") for h in range(HALVES)]
        x1_back = [sem(f"x1_back{i}") for i in range(4)]
        band_out = sem("band_out")
        bias_in = sem("bias_in")
        stored = sem("stored")
        masked_row = sem("masked_row")
        zeros_ready = sem("zeros_ready")
        w_hi, w_lo = sem("w_hi"), sem("w_lo")
        xg_hi, xg_lo = sem("xg_hi"), sem("xg_lo")
        squared, summed = sem("squared"), sem("summed")
        item_full, item_evac = sem("item_full"), sem("item_evac")
        root_ready = sem("root_ready")
        split_hi, split_lo = sem("split_hi"), sem("split_lo")
        window_step, pool_step = sem("window_step"), sem("pool_step")
        scores_full, logits_ready, negmax_ready = sem("scores_full"), sem("logits_ready"), sem("negmax_ready")
        exp_ready, denom_step, probs_ready = sem("exp_ready"), sem("denom_step"), sem("probs_ready")
        pt_full, pt_hi, pt_lo = sem("pt_full"), sem("pt_hi"), sem("pt_lo")
        heads_full, heads_hi, heads_lo = sem("heads_full"), sem("heads_hi"), sem("heads_lo")
        x1_step, x1_ready, x1_hi, x1_lo = sem("x1_step"), sem("x1_ready"), sem("x1_hi"), sem("x1_lo")
        gate_full, gate_evac, silu_ready, silu_scaled = (
            sem("gate_full"), sem("gate_evac"), sem("silu_ready"), sem("silu_scaled"))
        up_full, up_evac, hid_hi, hid_lo = sem("up_full"), sem("up_evac"), sem("hid_hi"), sem("hid_lo")
        down_full, down_evac = sem("down_full"), sem("down_evac")
        final_step, final_ready = sem("final_step"), sem("final_ready")

        PER_GROUP = 3 * FF_PER_GROUP

        def ring_slot(n):
            return n % RING

        def gate_up_slot(s):
            return (N_RING + s) % RING if s < RING else 3

        def weight_cols(n):
            return P if WEIGHTS[n][0] == "mix" else 1024

        def ring_source(n):
            kind, half, which = WEIGHTS[n]
            if kind == "mix":
                return w_pool[which]
            if kind == "out":
                return w_out_t[which]
            order = ("u0", "u1", "u2", "u3", "q0", "q1", "q2", "q3", "k", "v")
            return w_in_t[order.index(which)]

        block = ctx.enter_context(nc.Block())

        @block.sync
        def _(sp):
            def load_raw(n_parity, count, src, cols):
                sp.wait_ge(w_lo, count - RAW + 1)
                sp.dma_start(raw[:, n_parity, 0:cols], src).then_inc(raw_in[n_parity], 16)

            sp.dma_start(sm[:, :], small).then_inc(small_in, 16)
            sp.dma_start(raw[:, 0, :], ring_source(0)).then_inc(raw_in[0], 16)
            for c in range(2):
                sp.dma_start(big[:, 0, 4 * c:4 * c + 4, :], x_t[0, :, 4 * c:4 * c + 4, :]).then_inc(x_in[c], 16)
            sp.dma_start(raw[:, 1, :], ring_source(1)).then_inc(raw_in[1], 16)
            sp.dma_start(cst[:, :], consts).then_inc(small_in, 16)
            sp.dma_start(rel_sb[0:N_BUCKETS, :], rel).then_inc(small_in, 16)
            sp.dma_start(sum_mix[0:N_BUCKETS + 1, 0:BAND], onehot).then_inc(onehot_in, 16)
            for n in range(RAW, N_RING):
                if n == 3:
                    for c in range(2):
                        sp.dma_start(big[:, 1, 4 * c:4 * c + 4, :], x_t[1, :, 4 * c:4 * c + 4, :]).then_inc(x_in[2 + c], 16)
                load_raw(n % RAW, n, ring_source(n), weight_cols(n))

            def load_group(g, with_gate_up=True, with_down=True):
                if with_gate_up:
                    for s in range(2 * FF_PER_GROUP):
                        w = w_up_t if s % 2 else w_gate_t
                        src = w[bass.ds(g * FF_PER_GROUP + s // 2, 1)].rearrange("a p n -> p (a n)")
                        load_raw(s % RAW, N_RING + PER_GROUP * g + s, src, 1024)
                if with_down:
                    for c in range(FF_PER_GROUP):
                        src = w_down[bass.ds(g * FF_PER_GROUP + c, 1)].rearrange("a p n -> p (a n)")
                        load_raw(c % RAW, N_RING + PER_GROUP * g + 4 + c, src, 1024)

            with sp.Fori(0, GROUPS) as g:
                load_group(g)

            sp.wait_ge(item_evac, EVAC[("norm", "x1", 1)])
            for h in range(HALVES):
                sp.wait_ge(spilled[h], 16 * KD)
            for z in range(4):
                sp.dma_start(late[:, z, :], x1_spill[z // KD, :, z % KD, :]).then_inc(x1_back[z], 16)
            for z in range(HALVES * KD):
                sp.wait_ge(final_ready, z + 1)
                sp.dma_start(out_t[z // KD, :, z % KD, :], big[:, z // KD, z % KD, :]).then_inc(stored, 16)
                y = z + 4
                if y < HALVES * KD:
                    sp.dma_start(late[:, y % 4, :], x1_spill[y // KD, :, y % KD, :]).then_inc(x1_back[y % 4], 16)
            sp.wait_ge(stored, 16 * HALVES * KD)

        @block.gpsimd
        def _(pool):
            def weights_lo(dst_hi, dst_lo, parity, n, cols=1024):
                pool.wait_ge(w_hi, n + 1)
                nc.gpsimd.tensor_tensor(dst_lo[:, 0:cols], raw[:, parity, 0:cols], dst_hi[:, 0:cols].bitcast(F32),
                                        ALU.subtract).then_inc(w_lo, 1)

            def add_square(s):
                if s[2] == 0:
                    return
                pool.wait_ge(squared, SQUARE_NO[s])
                if ADD_NO[s] > 1:
                    pool.wait_ge(summed, ADD_NO[s] - 1)
                acc = sum_at(s[0], s[1])
                nc.gpsimd.tensor_tensor(acc, acc, square_at(s), ALU.add).then_inc(summed, 1)

            for e in TIMELINE:
                if e[0] == "weights":
                    n = e[1]
                    if n < N_RING:
                        s = ring_slot(n)
                        weights_lo(slots[:, s, HI, :], slots[:, s, LO, :], n % RAW, n, weight_cols(n))
                    else:
                        s = gate_up_slot(n - N_RING)
                        weights_lo(slots[:, s, HI, :], slots[:, s, LO, :], n % RAW, n)
                elif e[0] == "xsquares":
                    for k in range(KD):
                        add_square(("x", e[1], k))
                elif e[0] == "square":
                    add_square(e[1:])
                elif e[0] == "residual":
                    add_square(("x1", e[1], e[2]))
                elif e[0] == "evac" and e[1][0] == "proj" and e[1][2][0] == "u":
                    half, g = e[1][1], int(e[1][2][1])
                    pool.wait_ge(item_evac, EVAC[e[1]])
                    src = u_buf
                    for i in range(g + 1):
                        lo, shift, dst = 2 ** (i + 1) - 1, 2 ** i, win[i % 2]
                        done = WINDOW_STEPS[(half, g)] - (g + 1) + i
                        if done > 0:
                            pool.wait_ge(window_step, done)
                        nc.gpsimd.tensor_tensor(dst[:, lo:], src[:, lo:], src[:, lo - shift:HIST + T - shift],
                                                ALU.add).then_inc(window_step, 1)
                        src = dst

            def down_weights(g):
                for c in range(FF_PER_GROUP):
                    weights_lo(wd[:, c, HI, :], wd[:, c, LO, :], c % RAW, N_RING + PER_GROUP * g + 4 + c)

            def gate_up_weights(g):
                for s in range(2 * FF_PER_GROUP):
                    at = gate_up_slot(s)
                    weights_lo(slots[:, at, HI, :], slots[:, at, LO, :], s % RAW, N_RING + PER_GROUP * g + s)

            down_weights(0)
            for t in range(KD):
                add_square(("x1", 1, t))
            gate_up_weights(1)
            with pool.Fori(1, GROUPS - 1) as g:
                down_weights(g)
                gate_up_weights(g + 1)
            down_weights(GROUPS - 1)
            for h in range(HALVES):
                for t in range(KD):
                    add_square(("f", h, t))

        @block.scalar
        def _(act):
            def weights_hi(dst, parity, n, cols=1024):
                act.wait_ge(raw_in[parity], 16 * (n // RAW + 1) if isinstance(n, int) else n)
                nc.scalar.copy(dst[:, 0:cols], raw[:, parity, 0:cols]).then_inc(w_hi, 1)

            def square(s, src):
                no = SQUARES.index(s)
                if s[2] == 0:
                    if s[0] in ("mix", "f") and s[1:] != (0, 0) or s == ("x1", 1, 0):
                        last = {("mix", 1): ("norm", "mix", 0), ("x1", 1): ("norm", "x1", 0),
                                ("f", 1): ("norm", "f", 0)}[s[:2]]
                        act.wait_ge(item_full, FULL[last])
                    elif s[:2] == ("f", 0):
                        act.wait_ge(item_full, FULL[("norm", "mix", 1)])
                else:
                    same = [r for r in SQUARES[:no] if r[2] > 0 and square_place(r) == square_place(s)]
                    if same:
                        act.wait_ge(summed, ADD_NO[same[-1]])
                nc.scalar.activation(square_at(s), src, ACT.Square).then_inc(squared, 1)

            def square_place(r):
                return ("x", r[2] % 2) if r[0] == "x" else ("x1",) if r[0] == "x1" else ("tmp",)

            def norm_root(item):
                act.wait_ge(item_full, FULL[item])
                nc.scalar.activation(rms[:, item[2], :], ps[:, BANK[item], :], ACT.Sqrt, bias=eps_col,
                                     scale=1.0 / D).then_inc(root_ready, 1)

            def residual_hi(h, t):
                z = KD * h + t
                act.wait_ge(x1_ready, z + 1)
                nc.scalar.activation(mov[:, HI, h, t, :], big[:, h, t, :], ACT.Copy,
                                     scale=sm[:, G_PRE_FFN + t:G_PRE_FFN + t + 1]).then_inc(x1_hi, 1)
                square(("x1", h, t), big[:, h, t, :])
                act.dma_start(x1_spill[h, :, t, :], big[:, h, t, :]).then_inc(spilled[h], 16)
                if t + 2 < KD:
                    load_x(h, t + 2)

            def load_x(h, t):
                z = KD * h + t
                act.dma_start(late[:, z % 2, :], x_t[h, :, t, :]).then_inc(x_again[z % 2], 16)

            eps_col = cst[:, N_CONST - 1:N_CONST]
            act.wait_ge(small_in, 48)
            for e in TIMELINE:
                kind = e[0]
                if kind == "weights":
                    n = e[1]
                    if n < N_RING:
                        if n >= RING:
                            act.wait_ge(item_full, FULL[WEIGHTS[n - RING]])
                        weights_hi(slots[:, ring_slot(n), HI, :], n % RAW, n, weight_cols(n))
                    else:
                        s = n - N_RING
                        if s < RING:
                            act.wait_ge(item_full, FULL[WEIGHTS[N_RING + s - RING]])
                        else:
                            act.wait_ge(heads_full, UNITS)
                        weights_hi(slots[:, gate_up_slot(s), HI, :], n % RAW, n)
                elif kind == "xsplit":
                    h = e[1]
                    for k in range(KD):
                        act.wait_ge(x_in[2 * h + k // 4], 16)
                        nc.scalar.activation(mov[:, HI, h, k, :], big[:, h, k, :], ACT.Copy,
                                             scale=sm[:, G_PRE_MIX + k:G_PRE_MIX + k + 1]).then_inc(xg_hi, 1)
                elif kind == "xsquares":
                    for k in range(KD):
                        square(("x", e[1], k), big[:, e[1], k, :])
                elif kind == "square":
                    what, h, t = e[1:]
                    act.wait_ge(item_evac, EVAC[("out", h, t)])
                    square((what, h, t), big[:, h, t, :])
                elif kind == "bias_read":
                    act.wait_ge(band_out, 16)
                    rows = bass.AP(tensor=band_rows.tensor, offset=0, ap=[[1, P], [BAND, N_HEADS], [1, 256]])
                    act.dma_start(bias8[:, :].rearrange("p (h k) -> p h k", h=N_HEADS), rows).then_inc(bias_in, 16)
                elif kind == "pool_split":
                    _, h, g = e
                    if h == 1:
                        act.wait_ge(item_evac, EVAC[("proj", 1, "q3")])
                    else:
                        act.wait_ge(item_evac, EVAC[("proj", 0, "q3")])
                    act.wait_ge(pool_step, POOL_STEPS[(h, g)])
                    nc.scalar.copy(mov[:, HI, h, g, :], pooled[:, g, :]).then_inc(split_hi, 1)
                elif kind == "exp":
                    u = e[1]
                    b = u % 2
                    act.wait_ge(negmax_ready, u + 1)
                    nc.scalar.activation(stat[:, b, 3, :], stat[:, b, 2, :], ACT.Exp)
                    k0 = 256 - BLOCK * len(key_blocks(u))
                    for i in range(4):
                        at = lbuf[:, b, 256 * i + k0:256 * i + 256]
                        last = nc.scalar.activation(at, at, ACT.Exp, bias=stat[:, b, 1, i:i + 1],
                                                    accum_out=stat[:, b, 4, i:i + 1])
                    last.then_inc(exp_ready, 1)
                elif kind == "heads_out":
                    u = e[1]
                    h, jp, blk = unit_place(u)
                    act.wait_ge(heads_full, u + 1)
                    dst = mov[:, HI, h, 4 + 2 * jp:6 + 2 * jp, BLOCK * (blk % 4):BLOCK * (blk % 4 + 1)]
                    src = ps[:, 2 * (u % 2), 0:256].rearrange("p (j t) -> p j t", j=2)
                    nc.scalar.copy(dst, src).then_inc(heads_hi, 1)
                elif kind == "probs_split":
                    u = e[1]
                    if u >= 1:
                        act.wait_ge(heads_full, u)
                    for kb in key_blocks(u):
                        act.wait_ge(pt_full, PT_COUNT[u] - 1 + kb)
                        nc.scalar.copy(probs_t[:, HI, 512 * kb:512 * kb + 512], ps[:, 4 + kb, :]).then_inc(pt_hi, 1)
                elif kind == "x_load":
                    act.wait_ge(logits_ready, UNITS)
                    load_x(e[1], e[2])
                elif kind == "residual":
                    residual_hi(e[1], e[2])
                elif kind == "evac":
                    item = e[1]
                    if item[0] == "norm":
                        norm_root(item)
                    elif item[0] == "bias":
                        act.wait_ge(item_evac, EVAC[item])
                        act.dma_start(band_rows, band_sb).then_inc(band_out, 16)
                    elif item[0] == "vtr":
                        act.wait_ge(item_full, FULL[item])
                        h = item[1]
                        dst = vv[:, HI, 4 * h:4 * h + 4, :].rearrange("p b (c d) -> p b c d", d=64)[:, :, 0:3:2, :]
                        src = ps[:, BANK[item], :].rearrange("p (b c d) -> p b c d", b=4, c=2)
                        nc.scalar.copy(dst, src).then_inc(split_hi, 1)
                    elif item[0] == "mix":
                        _, h, g = item
                        act.wait_ge(item_full, FULL[item])
                        nc.scalar.activation(mov[:, HI, h, g, :], ps[:, BANK[item], :], ACT.Copy,
                                             scale=sm[:, POOL_SCALE + g:POOL_SCALE + g + 1]).then_inc(split_hi, 1)
                    elif item[0] == "proj" and item[2][0] == "q":
                        act.wait_ge(item_evac, EVAC[item])
                        nc.scalar.copy(q[:, int(item[2][1]), HI, :], tmp[:, :]).then_inc(split_hi, 1)
                    elif item[0] == "proj" and item[2] == "k":
                        act.wait_ge(item_evac, EVAC[item])
                        for v in range(N_KV):
                            rows = slice(64 * v, 64 * v + 64)
                            last = nc.scalar.copy(kk[rows, HI, v, T * item[1]:T * (item[1] + 1)], tmp[rows, :])
                        last.then_inc(split_hi, 1)

            def down_weights(g):
                act.wait_ge(down_full, 16 * g)
                for c in range(FF_PER_GROUP):
                    wait_raw(c % RAW, g, 4 + c)
                    nc.scalar.copy(wd[:, c, HI, :], raw[:, c % RAW, :]).then_inc(w_hi, 1)

            def wait_raw(parity, g, c):
                act.wait_ge(raw_in[parity], 16 * ((N_RING + c) // RAW + 1) + 16 * (PER_GROUP // RAW) * g)

            def gate_up_weight(g, s):
                act.wait_ge(up_full if s % 2 else gate_full, 4 * g - 1 + s // 2)
                wait_raw(s % RAW, g, s)
                nc.scalar.copy(slots[:, gate_up_slot(s), HI, :], raw[:, s % RAW, :]).then_inc(w_hi, 1)

            def silu(g, i):
                act.wait_ge(gate_evac, 4 * g + i + 1)
                nc.scalar.activation(lq[:, 1, :], lq[:, 0, :], ACT.Silu).then_inc(silu_ready, 1)

            def hidden_hi(g, i):
                act.wait_ge(up_evac, 4 * g + i + 1)
                nc.scalar.copy(hid[:, i % 2, HI, T * (i // 2):T * (i // 2) + T], lq[:, 2, :]).then_inc(hid_hi, 1)

            def group(g, first=False, last=False):
                silu(g, 0)
                hidden_hi(g, 0)
                if first:
                    for c in range(FF_PER_GROUP):
                        wait_raw(c % RAW, 0, 4 + c)
                        nc.scalar.copy(wd[:, c, HI, :], raw[:, c % RAW, :]).then_inc(w_hi, 1)
                    for t in range(KD // 2):
                        residual_hi(1, t)
                else:
                    down_weights(g)
                silu(g, 1)
                hidden_hi(g, 1)
                if first:
                    for t in range(KD // 2, KD):
                        residual_hi(1, t)
                    norm_root(("norm", "x1", 1))
                silu(g, 2)
                if not last:
                    gate_up_weight(g + 1, 0)
                hidden_hi(g, 2)
                if not last:
                    gate_up_weight(g + 1, 1)
                silu(g, 3)
                if not last:
                    gate_up_weight(g + 1, 2)
                hidden_hi(g, 3)
                if not last:
                    gate_up_weight(g + 1, 3)

            norm_root(("norm", "x1", 0))
            norm_root(("norm", "mix", 1))
            act.wait_ge(x1_ready, KD)
            load_x(1, 0)
            load_x(1, 1)
            group(0, first=True)
            with act.Fori(1, GROUPS - 1) as g:
                group(g)
            group(GROUPS - 1, last=True)
            for h in range(HALVES):
                for t in range(KD):
                    act.wait_ge(down_evac, 16 * (GROUPS - 1) + KD * h + t + 1)
                    square(("f", h, t), big[:, h, t, :])
                norm_root(("norm", "f", h))

        @block.vector
        def _(dve):
            steps = {"pool": 0}
            tmp_read = {"lo": 0}

            def norm_reciprocal(item):
                dve.wait_ge(root_ready, NORM_NO[item])
                r = rms[:, item[2], :]
                nc.vector.reciprocal(r, r).then_inc(item_evac, 1)

            def residual(h, t):
                z = KD * h + t
                at = big[:, h, t, :]
                if t == 0:
                    dve.wait_ge(item_evac, EVAC[("norm", "mix", h)])
                nc.vector.tensor_tensor(at, at, rms[:, h, :], ALU.mult).then_inc(x1_step, 1)
                dve.wait_ge(x_again[z % 2], 16 * (z // 2 + 1))
                dve.wait_ge(x1_step, z + 1)
                nc.vector.scalar_tensor_tensor(out=at, in0=at, scalar=sm[:, G_POST_MIX + t:G_POST_MIX + t + 1],
                                               in1=late[:, z % 2, :], op0=ALU.mult, op1=ALU.add).then_inc(x1_ready, 1)
                dve.wait_ge(x1_hi, z + 1)
                nc.vector.scalar_tensor_tensor(out=mov[:, LO, h, t, :], in0=at,
                                               scalar=sm[:, G_PRE_FFN + t:G_PRE_FFN + t + 1],
                                               in1=mov[:, HI, h, t, :].bitcast(F32), op0=ALU.mult,
                                               op1=ALU.subtract).then_inc(x1_lo, 1)

            nc.vector.memset(rel_sb[N_BUCKETS:N_BUCKETS + 1, :], MASKED).then_inc(masked_row, 1)
            nc.vector.memset(kk[64:128, :, 0, :].bitcast(F32), 0.0)
            nc.vector.memset(kk[0:64, :, 1, :].bitcast(F32), 0.0)
            nc.vector.memset(vv[:, :, :, 64:128].bitcast(F32), 0.0).then_inc(zeros_ready, 1)
            dve.wait_ge(small_in, 48)
            for e in TIMELINE:
                kind = e[0]
                if kind == "xsplit":
                    h = e[1]
                    for k in range(KD):
                        dve.wait_ge(xg_hi, KD * h + k + 1)
                        nc.vector.scalar_tensor_tensor(
                            out=mov[:, LO, h, k, :], in0=big[:, h, k, :], scalar=sm[:, G_PRE_MIX + k:G_PRE_MIX + k + 1],
                            in1=mov[:, HI, h, k, :].bitcast(F32), op0=ALU.mult, op1=ALU.subtract).then_inc(xg_lo, 1)
                elif kind == "pool":
                    _, h, g = e
                    w = WINDOWS[g]
                    s = win[g % 2]
                    dve.wait_ge(window_step, WINDOW_STEPS[(h, g)])
                    if steps["pool"]:
                        dve.wait_ge(pool_step, steps["pool"])
                    if (h, g) == (1, 0):
                        dve.wait_ge(split_lo, LO_NO[("pool_split", 0, 3)])
                    nc.vector.scalar_tensor_tensor(out=pooled[:, g, :], in0=s[:, HIST:], scalar=1.0 / w, in1=u_buf[:, HIST:],
                                                   op0=ALU.mult, op1=ALU.subtract).then_inc(pool_step, 1)
                    steps["pool"] += 1
                    if h == 0:
                        nc.vector.tensor_tensor(fix[:, 0:w - 1], s[:, HIST:HIST + w - 1],
                                                cst[:, INV_COUNT:INV_COUNT + w - 1], ALU.mult).then_inc(pool_step, 1)
                        steps["pool"] += 1
                        dve.wait_ge(pool_step, steps["pool"])
                        nc.vector.tensor_tensor(pooled[:, g, 0:w - 1], fix[:, 0:w - 1], u_buf[:, HIST:HIST + w - 1],
                                                ALU.subtract).then_inc(pool_step, 1)
                        nc.vector.tensor_copy(tails[:, g, :], u_buf[:, T:T + HIST]).then_inc(pool_step, 1)
                        steps["pool"] += 2
                    assert steps["pool"] == POOL_STEPS[(h, g)]
                elif kind == "pool_split":
                    _, h, g = e
                    dve.wait_ge(split_hi, SPLITS[e])
                    nc.vector.tensor_tensor(mov[:, LO, h, g, :], pooled[:, g, :], mov[:, HI, h, g, :].bitcast(F32),
                                            ALU.subtract).then_inc(split_lo, 1)
                elif kind == "logits":
                    u = e[1]
                    _, jp, _ = unit_place(u)
                    b = u % 2
                    k0 = 256 - BLOCK * len(key_blocks(u))
                    if u == 0:
                        dve.wait_ge(bias_in, 16)
                    dve.wait_ge(scores_full, u + 1)
                    for i in range(4):
                        head = 4 * jp + i
                        last = nc.vector.tensor_tensor_reduce(
                            out=lbuf[:, b, 256 * i + k0:256 * i + 256], in0=scores_of(u, i // 2)[:, i % 2, k0:256],
                            in1=bias8[:, 256 * head + k0:256 * head + 256], scale=SCALE,
                            scalar=sm[:, SINKS + head:SINKS + head + 1], op0=ALU.add, op1=ALU.max,
                            accum_out=stat[:, b, 0, i:i + 1])
                    last.then_inc(logits_ready, 1)
                    dve.wait_ge(logits_ready, u + 1)
                    sinks = sm[:, SINKS + 4 * jp:SINKS + 4 * jp + 4]
                    nc.vector.tensor_tensor(stat[:, b, 2, :], sinks, stat[:, b, 0, :], ALU.subtract)
                    nc.vector.tensor_scalar(stat[:, b, 1, :], stat[:, b, 0, :], -1.0, None, ALU.mult).then_inc(negmax_ready, 1)
                elif kind == "normalise":
                    u = e[1]
                    b = u % 2
                    k0 = 256 - BLOCK * len(key_blocks(u))
                    dve.wait_ge(exp_ready, u + 1)
                    nc.vector.tensor_tensor(stat[:, b, 5, :], stat[:, b, 3, :], stat[:, b, 4, :],
                                            ALU.add).then_inc(denom_step, 1)
                    dve.wait_ge(denom_step, 2 * u + 1)
                    nc.vector.reciprocal(stat[:, b, 6, :], stat[:, b, 5, :]).then_inc(denom_step, 1)
                    dve.wait_ge(denom_step, 2 * u + 2)
                    for i in range(4):
                        at = lbuf[:, b, 256 * i + k0:256 * i + 256]
                        last = nc.vector.tensor_scalar(at, at, stat[:, b, 6, i:i + 1], None, ALU.mult)
                    last.then_inc(probs_ready, 1)
                elif kind == "heads_out":
                    u = e[1]
                    h, jp, blk = unit_place(u)
                    dve.wait_ge(heads_hi, u + 1)
                    at = (h, slice(4 + 2 * jp, 6 + 2 * jp), slice(BLOCK * (blk % 4), BLOCK * (blk % 4 + 1)))
                    nc.vector.tensor_tensor(mov[:, LO, at[0], at[1], at[2]],
                                            ps[:, 2 * (u % 2), 0:256].rearrange("p (j t) -> p j t", j=2),
                                            mov[:, HI, at[0], at[1], at[2]].bitcast(F32), ALU.subtract).then_inc(heads_lo, 1)
                elif kind == "probs_split":
                    u = e[1]
                    for kb in key_blocks(u):
                        dve.wait_ge(pt_hi, PT_COUNT[u] - 1 + kb)
                        nc.vector.tensor_tensor(probs_t[:, LO, 512 * kb:512 * kb + 512], ps[:, 4 + kb, :],
                                                probs_t[:, HI, 512 * kb:512 * kb + 512].bitcast(F32),
                                                ALU.subtract).then_inc(pt_lo, 1)
                elif kind == "residual":
                    residual(e[1], e[2])
                elif kind == "evac":
                    item = e[1]
                    bank = ps[:, BANK[item], :]
                    if item[0] == "norm":
                        norm_reciprocal(item)
                    elif item[0] == "bias":
                        dve.wait_ge(item_full, FULL[item])
                        nc.vector.tensor_scalar(band_sb, bank[0:N_HEADS, 0:BAND], 1.0 / SCALE, None,
                                                ALU.mult).then_inc(item_evac, 1)
                    elif item[0] == "out":
                        dve.wait_ge(item_full, FULL[item])
                        nc.vector.tensor_copy(big[:, item[1], item[2], :], bank).then_inc(item_evac, 1)
                    elif item[0] == "mix":
                        _, h, g = item
                        dve.wait_ge(split_hi, SPLITS[item])
                        nc.vector.scalar_tensor_tensor(
                            out=mov[:, LO, h, g, :], in0=bank, scalar=sm[:, POOL_SCALE + g:POOL_SCALE + g + 1],
                            in1=mov[:, HI, h, g, :].bitcast(F32), op0=ALU.mult, op1=ALU.subtract).then_inc(item_evac, 1)
                    elif item[0] == "vtr":
                        h = item[1]
                        dve.wait_ge(split_hi, SPLITS[item])
                        at = [vv[:, s, 4 * h:4 * h + 4, :].rearrange("p b (c d) -> p b c d", d=64)[:, :, 0:3:2, :]
                              for s in (HI, LO)]
                        nc.vector.tensor_tensor(at[1], bank.rearrange("p (b c d) -> p b c d", b=4, c=2),
                                                at[0].bitcast(F32), ALU.subtract).then_inc(item_evac, 1)
                    elif item[0] == "proj":
                        h, name = item[1:]
                        dve.wait_ge(item_full, FULL[item])
                        dve.wait_ge(item_evac, EVAC[("norm", "x", h)])
                        if name[0] == "u":
                            g = int(name[1])
                            if (h, g) == (0, 0):
                                dve.wait_ge(squared, SQUARE_NO[("x", 1, KD - 1)])
                                dve.wait_ge(xg_lo, HALVES * KD)
                            if steps["pool"]:
                                dve.wait_ge(pool_step, steps["pool"])
                            if h == 0:
                                if g == 0:
                                    nc.vector.memset(u_buf[:, 0:HIST], 0.0)
                            else:
                                nc.vector.tensor_copy(u_buf[:, 0:HIST], tails[:, g, :])
                            nc.vector.tensor_tensor(u_buf[:, HIST:], bank, rms[:, h, :], ALU.mult).then_inc(item_evac, 1)
                        else:
                            if item == ("proj", 0, "k"):
                                dve.wait_ge(onehot_in, 16)
                            if tmp_read["lo"]:
                                dve.wait_ge(split_lo, tmp_read["lo"])
                            dst, src, r = tmp[:, :], bank, rms[:, h, :]
                            if name[0] == "q":
                                dst = dst.rearrange("p (b t) -> p b t", b=4)[:, :, ::-1]
                                src, r = (a.rearrange("p (b t) -> p b t", b=4) for a in (src, r))
                            nc.vector.tensor_tensor(dst, src, r, ALU.mult).then_inc(item_evac, 1)
                            if name != "v":
                                tmp_read["lo"] = LO_NO[item]
                            if name[0] == "q":
                                dve.wait_ge(split_hi, SPLITS[item])
                                j = int(name[1])
                                nc.vector.tensor_tensor(q[:, j, LO, :], tmp[:, :], q[:, j, HI, :].bitcast(F32),
                                                        ALU.subtract).then_inc(split_lo, 1)
                            elif name == "k":
                                dve.wait_ge(split_hi, SPLITS[item])
                                for v in range(N_KV):
                                    rows, cols = slice(64 * v, 64 * v + 64), slice(T * h, T * h + T)
                                    last = nc.vector.tensor_tensor(kk[rows, LO, v, cols], tmp[rows, :],
                                                                   kk[rows, HI, v, cols].bitcast(F32), ALU.subtract)
                                last.then_inc(split_lo, 1)

            def gate_out(g, i):
                dve.wait_ge(gate_full, 4 * g + i + 1)
                nc.vector.tensor_tensor(lq[:, 0, :], ps[:, 2 * (i % 2), :], rms[:, i // 2, :], ALU.mult).then_inc(gate_evac, 1)
                dve.wait_ge(silu_ready, 4 * g + i + 1)
                nc.vector.tensor_tensor(lq[:, 3, :], lq[:, 1, :], rms[:, i // 2, :], ALU.mult).then_inc(silu_scaled, 1)

            def up_out(g, i):
                dve.wait_ge(up_full, 4 * g + i + 1)
                dve.wait_ge(silu_scaled, 4 * g + i + 1)
                if not (isinstance(g, int) and g == 0 and i == 0):
                    dve.wait_ge(hid_lo, 4 * g + i)
                nc.vector.tensor_tensor(lq[:, 2, :], ps[:, 2 * (i % 2) + 1, :], lq[:, 3, :], ALU.mult).then_inc(up_evac, 1)
                dve.wait_ge(hid_hi, 4 * g + i + 1)
                cols = slice(T * (i // 2), T * (i // 2) + T)
                nc.vector.tensor_tensor(hid[:, i % 2, LO, cols], lq[:, 2, :], hid[:, i % 2, HI, cols].bitcast(F32),
                                        ALU.subtract).then_inc(hid_lo, 1)

            def add_down(g, e, first=False):
                h, t = e // KD, e % KD
                if first and t == 0:
                    dve.wait_ge(spilled[h], 16 * KD)
                dve.wait_ge(down_full, 16 * g + e + 1)
                at, bank = big[:, h, t, :], ps[:, 4 + e % 4, :]
                if first:
                    nc.vector.tensor_copy(at, bank).then_inc(down_evac, 1)
                else:
                    nc.vector.tensor_tensor(at, at, bank, ALU.add).then_inc(down_evac, 1)

            def group(g, first=False):
                for i in range(4):
                    if first and i == 2:
                        norm_reciprocal(("norm", "x1", 1))
                    if first and i in (0, 2):
                        dve.wait_ge(item_evac, EVAC[("norm", "x1", i // 2)])
                    gate_out(g, i)
                    up_out(g, i)
                    if first and i < 2:
                        for t in range(4 * i, 4 * i + 4):
                            residual(1, t)

            def final(h, t):
                z = KD * h + t
                at = big[:, h, t, :]
                nc.vector.tensor_tensor(at, at, rms[:, h, :], ALU.mult).then_inc(final_step, 1)
                dve.wait_ge(x1_back[z % 4], 16 * (z // 4 + 1))
                dve.wait_ge(final_step, z + 1)
                nc.vector.scalar_tensor_tensor(out=at, in0=at, scalar=sm[:, G_POST_FFN + t:G_POST_FFN + t + 1],
                                               in1=late[:, z % 4, :], op0=ALU.mult, op1=ALU.add).then_inc(final_ready, 1)

            norm_reciprocal(("norm", "x1", 0))
            norm_reciprocal(("norm", "mix", 1))
            group(0, first=True)
            for e in range(16):
                add_down(0, e, first=True)
            with dve.Fori(1, GROUPS - 1) as g:
                group(g)
                for e in range(16):
                    add_down(g, e)
            g = GROUPS - 1
            group(g)
            for e in range(12):
                add_down(g, e)
            norm_reciprocal(("norm", "f", 0))
            dve.wait_ge(item_evac, EVAC[("norm", "f", 0)])
            for e in range(12, 16):
                add_down(g, e)
            for t in range(KD):
                final(0, t)
            norm_reciprocal(("norm", "f", 1))
            dve.wait_ge(item_evac, EVAC[("norm", "f", 1)])
            for t in range(KD):
                final(1, t)

        @block.tensor
        def _(pe):
            def product(out, w, x, start, stop):
                nc.tensor.matmul(out, w[HI], x[HI], start=start, stop=False)
                nc.tensor.matmul(out, w[HI], x[LO], start=False, stop=False)
                return nc.tensor.matmul(out, w[LO], x[HI], start=False, stop=stop)

            def weight(s, k):
                return [slots[:, s, part, P * k:P * k + P] for part in (HI, LO)]

            def moving(h, k):
                return [mov[:, part, h, k, :] for part in (HI, LO)]

            def norm_sum(item, banks_free=None):
                what, h = item[1:]
                pe.wait_ge(summed, ADD_NO[(what, h, KD - 1)])
                bank_free(item)
                nc.tensor.matmul(ps[:, BANK[item], :], ones, sum_at(what, h), start=True, stop=True).then_inc(item_full, 1)

            def bank_free(item):
                if BANK_BEFORE[item] is not None:
                    pe.wait_ge(item_evac, EVAC[BANK_BEFORE[item]])

            n = 0
            for item in PE_ORDER:
                kind = item[0]
                if kind in ("proj", "out", "mix"):
                    pe.wait_ge(w_lo, n + 1)
                    bank_free(item)
                    out, slot = ps[:, BANK[item], :], ring_slot(n)
                    if kind == "mix":
                        _, h, g = item
                        pe.wait_ge(split_lo, LO_NO[("pool_split", h, g)])
                        last = product(out, weight(slot, 0), moving(h, g), True, True)
                    else:
                        h = item[1]
                        if kind == "out":
                            pe.wait_ge(item_evac, EVAC[("mix", h, 3)])
                            pe.wait_ge(heads_lo, 8 * (h + 1))
                        for k in range(KD):
                            if kind == "proj":
                                pe.wait_ge(xg_lo, KD * h + k + 1)
                            last = product(out, weight(slot, k), moving(h, k), k == 0, k == KD - 1)
                    last.then_inc(item_full, 1)
                    n += 1
                elif kind == "norm":
                    if item == ("norm", "x", 0):
                        pe.wait_ge(small_in, 48)
                    norm_sum(item)
                elif kind == "bias":
                    pe.wait_ge(masked_row, 1)
                    pe.wait_ge(onehot_in, 16)
                    bank_free(item)
                    nc.tensor.matmul(ps[0:N_HEADS, BANK[item], 0:BAND], rel_sb[:, :], sum_mix[0:N_BUCKETS + 1, 0:BAND],
                                     start=True, stop=True).then_inc(item_full, 1)
                elif kind == "vtr":
                    pe.wait_ge(item_evac, EVAC[("proj", item[1], "v")])
                    bank_free(item)
                    for b in range(4):
                        last = nc.tensor.transpose(ps[:, BANK[item], P * b:P * b + P], tmp[:, P * b:P * b + P], ident)
                    last.then_inc(item_full, 1)
                elif kind == "scores":
                    u = item[1]
                    h, jp, blk = unit_place(u)
                    if u == 0:
                        pe.wait_ge(zeros_ready, 1)
                        pe.wait_ge(item_evac, max(EVAC[PRE_LAST[b]] for b in range(4)))
                    if u >= 2:
                        pe.wait_ge(heads_lo, u - 1)
                    pe.wait_ge(split_lo, max(LO_NO[("proj", h, n_)] for n_ in ("k", f"q{2 * jp}", f"q{2 * jp + 1}")))
                    nk = BLOCK * len(key_blocks(u))
                    keys = slice(BLOCK * (blk + 1) - nk, BLOCK * (blk + 1))
                    qs = slice(BLOCK * (blk % 4), BLOCK * (blk % 4 + 1))
                    for jj in range(2):
                        j = 2 * jp + jj
                        last = product(scores_of(u, jj)[:, :, 256 - nk:256], [q[:, j, p_, qs] for p_ in (HI, LO)],
                                       [kk[:, p_, :, keys] for p_ in (HI, LO)], True, True)
                    last.then_inc(scores_full, 1)
                elif kind == "transpose":
                    u = item[1]
                    pe.wait_ge(probs_ready, u + 1)
                    if u >= 1:
                        pe.wait_ge(pt_lo, PT_COUNT[u - 1])
                    for kb in key_blocks(u):
                        for v in range(N_KV):
                            for jj in range(2):
                                src = lbuf[:, u % 2, 256 * (2 * jj + v) + P * kb:256 * (2 * jj + v) + P * kb + P]
                                last = nc.tensor.transpose(ps[:, 4 + kb, P * (2 * v + jj):P * (2 * v + jj) + P], src, flip)
                        last.then_inc(pt_full, 1)
                elif kind == "values":
                    u = item[1]
                    h, jp, blk = unit_place(u)
                    pe.wait_ge(pt_lo, PT_COUNT[u])
                    pe.wait_ge(item_evac, EVAC[("vtr", h)])
                    out = ps[:, 2 * (u % 2), 0:256]
                    kbs = key_blocks(u)
                    for kb in kbs:
                        for v in range(N_KV):
                            last = product(out, [vv[:, p_, blk - 1 + kb, 64 * v:64 * v + P] for p_ in (HI, LO)],
                                           [probs_t[:, p_, 512 * kb + 256 * v:512 * kb + 256 * v + 256] for p_ in (HI, LO)],
                                           (kb, v) == (kbs[0], 0), (kb, v) == (1, 1))
                    last.then_inc(heads_full, 1)

            def gate(g, i, first=False):
                h, c = i // 2, i % 2
                out = ps[:, 2 * (i % 2), :]
                if not first or i >= 2:
                    pe.wait_ge(gate_evac, 4 * g + i - 1)
                else:
                    pe.wait_ge(heads_lo, UNITS)
                if h == 0:
                    pe.wait_ge(w_lo, N_RING + PER_GROUP * g + 2 * c + 1)
                for k in range(KD):
                    if first and c == 0:
                        pe.wait_ge(x1_lo, KD * h + k + 1)
                    last = product(out, weight(gate_up_slot(2 * c), k), moving(h, k), k == 0, k == KD - 1)
                    if first and i == 0 and k == 3:
                        norm_sum(("norm", "x1", 0))
                last.then_inc(gate_full, 1)

            def up(g, i, first=False):
                h, c = i // 2, i % 2
                out = ps[:, 2 * (i % 2) + 1, :]
                if not first or i >= 2:
                    pe.wait_ge(up_evac, 4 * g + i - 1)
                if h == 0:
                    pe.wait_ge(w_lo, N_RING + PER_GROUP * g + 2 * c + 2)
                for k in range(KD):
                    last = product(out, weight(gate_up_slot(2 * c + 1), k), moving(h, k), k == 0, k == KD - 1)
                last.then_inc(up_full, 1)

            def down(g, e, first=False):
                h, t = e // KD, e % KD
                if first and e < 4:
                    if e < 2:
                        pe.wait_ge(pt_lo, PT_COUNT[-1])
                    else:
                        pe.wait_ge(item_evac, EVAC[("norm", "x1", 1)])
                else:
                    pe.wait_ge(down_evac, 16 * g + e - 3)
                if t == 0:
                    pe.wait_ge(hid_lo, 4 * g + 2 * h + 2)
                if e == 0:
                    pe.wait_ge(w_lo, N_RING + PER_GROUP * g + 6)
                for c in range(FF_PER_GROUP):
                    last = product(ps[:, 4 + e % 4, :], [wd[:, c, p_, P * t:P * t + P] for p_ in (HI, LO)],
                                   [hid[:, c, p_, T * h:T * h + T] for p_ in (HI, LO)], c == 0, c == FF_PER_GROUP - 1)
                last.then_inc(down_full, 1)

            def group(g, first=False, last=False):
                for i in range(4):
                    gate(g, i, first)
                    if first and i == 0:
                        norm_sum(("norm", "mix", 1))
                    if first and i == 2:
                        norm_sum(("norm", "x1", 1))
                    up(g, i, first)
                for e in range(16):
                    down(g, e, first)
                    if last and e == 11:
                        pe.wait_ge(gate_evac, 4 * GROUPS)
                        norm_sum(("norm", "f", 0))

            group(0, first=True)
            with pe.Fori(1, GROUPS - 1) as g:
                group(g)
            group(GROUPS - 1, last=True)
            pe.wait_ge(up_evac, 4 * GROUPS)
            norm_sum(("norm", "f", 1))


POOL_STEPS, _n = {}, 0
for _e in TIMELINE:
    if _e[0] == "pool":
        _n += 4 if _e[1] == 0 else 1
        POOL_STEPS[_e[1:]] = _n
NORM_NO = {i: n + 1 for n, i in enumerate([i for i in EVACS if i[0] == "norm"])}
LO_NO = {s: n + 1 for n, s in enumerate(s for s in SPLITS if s[0] in ("proj", "pool_split"))}


def _shape_constants():
    consts = np.zeros((P, N_CONST), np.float32)
    consts[:, IDENT:IDENT + P] = np.eye(P, dtype=np.float32)
    consts[:, FLIP:FLIP + P] = np.eye(P, dtype=np.float32)[::-1]
    consts[:, ONES:ONES + P] = 1.0
    consts[:, INV_COUNT:INV_COUNT + HIST - 1] = 1.0 / np.arange(1, HIST, dtype=np.float32)
    consts[:, N_CONST - 1] = EPS
    exact = N_BUCKETS // 2
    dist = np.arange(BLOCK)
    near = np.maximum(dist, 1).astype(np.float32)
    large = exact + (np.log(near / np.float32(exact)) / np.float32(np.log(BLOCK / exact))
                     * np.float32(N_BUCKETS - exact)).astype(np.int32)
    bucket = np.where(dist < exact, dist, np.minimum(large, N_BUCKETS - 1))
    onehot = np.zeros((N_BUCKETS + 1, BAND), np.float32)
    for m in range(BAND):
        d = 2 * BLOCK - 1 - m
        onehot[bucket[d] if 0 <= d < BLOCK else N_BUCKETS, m] = 1.0
    return consts, onehot


def kernel(x, g_pre_mix, w_in, w_pool, pool_scale, rel_bias, sinks, w_out, g_post_mix, g_pre_ffn, w_gate, w_up,
           w_down, g_post_ffn):
    import concourse.bacc as bacc
    from concourse.bass_utils import run_bass_kernel_spmd

    def arr(a):
        return np.asarray(a)

    heads = [h for j in range(4) for h in (j, 4 + j)]
    x_t = np.ascontiguousarray(arr(x)[0].T.reshape(KD, P, HALVES, T).transpose(2, 1, 0, 3))
    cols = [np.arange(512)] + [512 + 64 * h + np.arange(64) for h in heads] + [np.arange(1024, 1280)]
    w_in_p = arr(w_in)[0][:, np.concatenate(cols)]

    def tiles(w):
        k, n = w.shape
        return np.ascontiguousarray(w.reshape(k // P, P, n // P, P).transpose(2, 1, 0, 3).reshape(n // P, P, k))

    rows = np.concatenate([np.arange(512)] + [512 + 64 * h + np.arange(64) for h in heads])
    small = np.concatenate(
        [arr(g)[0].reshape(KD, P).T for g in (g_pre_mix, g_post_mix, g_pre_ffn, g_post_ffn)]
        + [arr(pool_scale)[0].reshape(4, P).T, np.broadcast_to(arr(sinks)[0][heads], (P, N_HEADS))], axis=1)
    consts, onehot = _shape_constants()
    data = {
        "x_t": x_t,
        "small": np.ascontiguousarray(small),
        "consts": consts,
        "rel": np.ascontiguousarray(arr(rel_bias)[:, heads]),
        "onehot": onehot,
        "w_in_t": tiles(w_in_p),
        "w_pool": np.ascontiguousarray(arr(w_pool)[0]),
        "w_out_t": tiles(arr(w_out)[0][rows]),
        "w_gate_t": tiles(arr(w_gate)[0]),
        "w_up_t": tiles(arr(w_up)[0]),
        "w_down": np.ascontiguousarray(arr(w_down)[0].reshape(FF_TILES, P, D)),
    }
    nc = bacc.Bacc("TRN2", target_bir_lowering=False, num_devices=1)
    aps = [nc.dram_tensor(n, a.shape, mybir.dt.from_np(a.dtype), kind="ExternalInput").ap() for n, a in data.items()]
    out = nc.dram_tensor("out_t", [HALVES, P, KD, T], F32, kind="ExternalOutput").ap()
    hybrid_layer(nc, *aps, out)
    r = run_bass_kernel_spmd(nc, [data], core_ids=[0])
    got = np.asarray(r.results[0]["out_t"])
    return np.ascontiguousarray(got.transpose(0, 3, 2, 1).reshape(1, SEQ, D))
```

```python
from contextlib import ExitStack

import numpy as np

import concourse.bass as bass
from concourse import mybir

F32 = mybir.dt.float32
F32R = mybir.dt.float32r
ALU = mybir.AluOpType
ACT = mybir.ActivationFunctionType

P = 128
SEQ = 1024
D = 1024
HALVES = 2
T = SEQ // HALVES
KD = D // P
HEAD_DIM = 64
N_HEADS = 8
N_KV = 2
BLOCK = 128
BLOCKS = SEQ // BLOCK
WINDOWS = (2, 4, 8, 16)
HIST = 16
N_BUCKETS = 32
D_FF = 2816
FF_TILES = D_FF // P
FF_PER_GROUP = 2
GROUPS = FF_TILES // FF_PER_GROUP
EPS = 1e-6
MASKED = -1e30
SCALE = HEAD_DIM ** -0.5
BAND = 384

G_PRE_MIX, G_POST_MIX, G_PRE_FFN, G_POST_FFN, POOL_SCALE, SINKS = 0, 8, 16, 24, 32, 36
N_SMALL = 44
IDENT, FLIP, ONES, INV_COUNT = 0, 128, 256, 384
N_CONST = 384 + HIST

LO_BY_DVE = (0, 1, 42, 43, 44, 45)
WINDOWS_BY_DVE = ((0, "u0"), (0, "u1"))
RING = 3
RAW = 2
UNITS = 16
HI, LO = 0, 1


def unit_place(u):
    half = u // 8
    return half, (u // 4) % 2, 4 * half + u % 4


def key_blocks(u):
    return (1,) if unit_place(u)[2] == 0 else (0, 1)


def make_schedule():
    pre = [("proj", 0, "k"), ("proj", 0, "v"), ("norm", "x", 0), ("bias",), ("proj", 0, "q0"), ("vtr", 0),
           ("proj", 0, "q1"), ("proj", 0, "u0"), ("proj", 0, "u1"), ("proj", 0, "u2"), ("proj", 0, "u3"),
           ("norm", "x", 1), ("proj", 0, "q2"), ("proj", 0, "q3")]
    fill = {s: [("proj", 1, n)] for s, n in enumerate(("u0", "u1", "u2", "u3", "q0", "q1", "k", "v", "q2", "q3"))}
    for t in range(KD):
        fill[10 + t] = [("out", 0, t)]
    for g in range(4):
        fill[1 + g].append(("mix", 0, g))
        fill[11 + g].append(("mix", 1, g))
    pe = list(pre)
    for s in range(UNITS + 2):
        pe.append(fill[s][0] + ("values", s - 2) if s >= 2 else fill[s][0])
        pe += fill[s][1:]
        if s < UNITS:
            pe.append(("scores", s))
        if 1 <= s <= UNITS:
            pe.append(("transpose", s - 1))
        if s == 7:
            pe.append(("vtr", 1))
    pe += ([("out", 1, 0), ("norm", "mix", 0)] + [("out", 1, t) for t in range(1, KD)]
           + [("norm", "x1", 0)])
    weights = [i[:3] for i in pe if i[0] in ("proj", "mix", "out")]

    tl = [("weights", 0), ("xsplit", 0), ("weights", 1), ("xsquares", 0, range(4)), ("weights", 2),
          ("xsquares", 0, range(4, KD)), ("weights", 3), ("evac", ("norm", "x", 0)), ("weights", 4),
          ("evac", ("proj", 0, "k")), ("evac", ("proj", 0, "v")), ("split", 0, "k"), ("weights", 5),
          ("evac", ("bias",)), ("evac", ("vtr", 0)), ("evac", ("proj", 0, "q0")), ("split", 0, "q0"), ("bias_read",),
          ("evac", ("proj", 0, "q1")), ("weights", 6), ("split", 0, "q1"), ("xsplit", 1), ("weights", 7),
          ("xsquares", 1, range(KD))]
    tl += [("weights", 8), ("evac", ("proj", 0, "u0")), ("pool", 0, 0), ("weights", 9), ("evac", ("proj", 0, "u1")),
           ("pool", 0, 1), ("weights", 10), ("evac", ("proj", 0, "u2")), ("evac", ("norm", "x", 1)),
           ("evac", ("proj", 0, "q2")), ("split", 0, "q2"), ("weights", 11), ("pool", 0, 2),
           ("evac", ("proj", 0, "u3")), ("evac", ("proj", 0, "q3")), ("split", 0, "q3")]
    for s in range(UNITS + 2):
        if 1 <= s <= UNITS:
            tl += [("exp", s - 1), ("normalise", s - 1)]
        if s >= 2:
            tl.append(("heads_out", s - 2))
        tl += [("weights", weights.index(i) + 2) for i in fill[s][1 if s == 1 else 0:]]
        if 1 <= s <= 4:
            tl.append(("pool", 1, s - 1))
        if s == 0:
            tl += [("logits", 0), ("pool", 0, 3)]
        tl += [("evac", i) for i in fill[s]]
        if 0 < s < UNITS:
            tl.append(("logits", s))
        if s == 0:
            tl += [("pool_split", 0, 0), ("weights", weights.index(fill[1][0]) + 2), ("pool_split", 0, 1)]
        if 1 <= s <= UNITS:
            tl.append(("probs_split", s - 1))
        if s in (1, 2):
            tl.append(("pool_split", 0, s + 1))
        tl += [("split",) + i[1:] for i in fill[s] if i[0] == "proj" and i[2][0] in "qk"]
        tl += [("square", "mix", 0, i[2]) for i in fill[s] if i[0] == "out"]
        if s == 7:
            tl.append(("evac", ("vtr", 1)))
        if s >= 10 and s < 14:
            tl.append(("pool_split", 1, s - 10))
    first = weights.index(("out", 1, 0))
    tl += [("x_load", 0, 0), ("x_load", 0, 1), ("weights", first + 2), ("evac", ("out", 1, 0)), ("weights", first + 3),
           ("evac", ("norm", "mix", 0)), ("square", "mix", 1, 0), ("residual", 0, 0)]
    after = {1: (1, 2), 2: (3,), 3: (4, 5), 4: (6,), 5: (7,)}
    for t in range(1, KD):
        tl += [("evac", ("out", 1, t)), ("weights", first + t + 3)]
        tl += [("residual", 0, r) for r in after.get(t, ())]
        tl.append(("square", "mix", 1, t))
        if t == KD - 1:
            tl[-2:] = [("evac", ("norm", "x1", 0)), tl[-1], tl[-2], ("weights", len(weights) + 3)]
    return pre, pe, weights, tl


PRE, PE_ORDER, WEIGHTS, TIMELINE = make_schedule()
N_RING = len(WEIGHTS)
assert N_RING % RAW == 0
NORMS_FIRST = [("norm", "mix", 1), ("norm", "x1", 1)]
NORMS_LAST = [("norm", "f", 0), ("norm", "f", 1), ("norm", "f", 2)]
ITEMS = [i[:3] for i in PE_ORDER if i[0] in ("proj", "norm", "bias", "vtr", "mix", "out")] + NORMS_FIRST + NORMS_LAST
EVACS = [e[1] for e in TIMELINE if e[0] == "evac"] + NORMS_FIRST + NORMS_LAST
FULL = {i: n + 1 for n, i in enumerate(ITEMS)}
EVAC = {i: n + 1 for n, i in enumerate(EVACS)}
assert set(ITEMS) == set(EVACS) and len(ITEMS) == len(EVACS)


def make_banks():
    bank, before, last = {}, {}, {}
    n = 0
    for item in ITEMS:
        if item in PRE:
            b = (6, 7, 0, 1, 2, 3)[n % 6]
            n += 1
        elif item in NORMS_LAST or item == ("norm", "x1", 1):
            b = 4 if item[1] == "x1" else item[2]
            last.pop(b, None)
        else:
            b = 6 + n % 2
            n += 1
        bank[item] = b
        before[item] = last.get(b)
        last[b] = item
        if item == PRE[-1]:
            pre_last = dict(last)
    return bank, before, pre_last


BANK, BANK_BEFORE, PRE_LAST = make_banks()

SPLITS = {}
for _e in TIMELINE:
    if _e[0] == "evac" and _e[1][0] in ("vtr", "mix"):
        SPLITS[_e[1]] = len(SPLITS) + 1
    elif _e[0] == "split":
        SPLITS[("proj",) + _e[1:]] = len(SPLITS) + 1
    elif _e[0] == "pool_split":
        SPLITS[_e] = len(SPLITS) + 1

SQUARES = []
for _e in TIMELINE:
    if _e[0] == "xsquares":
        SQUARES += [("x", _e[1], k) for k in _e[2]]
    elif _e[0] == "square":
        SQUARES.append((_e[1], _e[2], _e[3]))
    elif _e[0] == "residual":
        SQUARES.append(("x1", _e[1], _e[2]))
SQUARES += [("x1", 1, t) for t in range(KD)]
SQUARES += [("f", part, t) for part in range(3) for t in range(KD)]
LAST_SUMMED_BY_PE = tuple(range(4, KD))
SQUARE_NO = {s: n + 1 for n, s in enumerate(SQUARES)}
ADD_NO, _n = {}, 0
for _s in SQUARES:
    _n += _s[2] > 0 and _s[0] != "x" and not (_s[:2] == ("f", 2) and _s[2] in LAST_SUMMED_BY_PE)
    ADD_NO[_s] = _n

PT_COUNT = [sum(len(key_blocks(v)) for v in range(u + 1)) for u in range(UNITS)]
PARTS = ((0, slice(0, T)), (1, slice(0, T // 2)), (1, slice(T // 2, T)))
SCALED_BY_DVE = ((), (0, 3, 6), (0, 5))


def scaled_by_pool(part, t):
    before = sum(KD - len(d) for d in SCALED_BY_DVE[:part])
    return before + sum(i not in SCALED_BY_DVE[part] for i in range(t + 1))


WINDOW_STEPS = {}
_n = 0
for _h in range(HALVES):
    for _g in range(4):
        _n += _g + 1
        WINDOW_STEPS[(_h, _g)] = _n


def hybrid_layer(nc, x_t, small, consts, rel, onehot, w_in_t, w_pool, w_out_t, w_gate_t, w_up_t, w_down, out_t):
    with ExitStack() as ctx:
        def sb(name, shape, dt=F32):
            return ctx.enter_context(nc.sbuf_tensor(name, shape, dt))

        def sem(name):
            return ctx.enter_context(nc.semaphore(name))

        band_rows = nc.dram_tensor("band_rows", [N_HEADS, BAND], F32, kind="Internal").ap()
        x1_spill = nc.dram_tensor("x1_spill", [HALVES, P, KD, T], F32, kind="Internal").ap()

        mov = sb("mov", [P, 2, HALVES, KD, T], F32R)
        slots = sb("slots", [P, 4, 2, 1024], F32R)
        probs_t = slots[:, 3, :, :]
        qd = sb("qd", [P, 4096], F32R)
        q = qd[:, :].rearrange("p (j v t) -> p j v t", j=4, v=2)
        wd = qd[:, :].rearrange("p (c s n) -> p c s n", c=2, s=2)
        kvb = sb("kvb", [P, 4096 + 2 * BLOCKS * 192], F32R)
        kk = kvb[:, 0:4096].rearrange("p (s v t) -> p s v t", s=2, v=2)
        vv = kvb[:, 4096:4096 + 2 * BLOCKS * 192].rearrange("p (s b d) -> p s b d", s=2, b=BLOCKS)
        hid = kvb[:, 0:4096].rearrange("p (c s t) -> p c s t", c=2, s=2)

        big = sb("big", [P, HALVES, KD, T])
        area = big[:, 1, :, :].rearrange("p k t -> p (k t)")
        u_buf = area[:, 0:HIST + T]
        win = [area[:, (1 + i) * (HIST + T):(2 + i) * (HIST + T)] for i in range(2)]
        pooled = area[:, 3 * (HIST + T):3 * (HIST + T) + 4 * T].rearrange("p (g t) -> p g t", g=4)
        tails = area[:, 3 * (HIST + T) + 4 * T:3 * (HIST + T) + 4 * T + 4 * HIST].rearrange("p (g t) -> p g t", g=4)
        raw = sb("raw", [P, RAW, 1024])
        bias8 = sb("bias8", [P, N_HEADS * 256])
        late = bias8[:, :].rearrange("p (s t) -> p s t", s=4)
        lbuf = sb("lbuf", [P, 2, 1024])
        lq = lbuf[:, :, :].rearrange("p b (s t) -> p (b s) t", s=2)
        tmp = sb("tmp", [P, T])
        sum_mix = sb("sum_mix", [P, T])
        rms = sb("rms", [P, HALVES, T])
        sm = sb("sm", [P, N_SMALL])
        cst = sb("cst", [P, N_CONST])
        stat = sb("stat", [P, 2, 7, 4])
        fix = sb("fix", [P, HIST])
        rel_sb = sb("rel_sb", [N_BUCKETS + 1, N_HEADS])

        band_sb = bias8[0:N_HEADS, 0:BAND]
        ident, flip, ones = cst[:, IDENT:IDENT + P], cst[:, FLIP:FLIP + P], cst[:, ONES:ONES + P]

        ps = ctx.enter_context(nc.psum_tensor("ps", [P, 8, 512], F32))

        def scores_of(u, jj):
            return ps[:, 2 * (u % 2) + jj, :].rearrange("p (v k) -> p v k", v=2)

        def square_at(s):
            what, half, k = s
            if k == 0:
                return sum_at(what, half)
            if what == "x":
                return lq[:, k % 2, :]
            if what == "f":
                width = PARTS[half][1].stop - PARTS[half][1].start
                if half == 2 and k in LAST_SUMMED_BY_PE:
                    return (lq[:, 1, 0:width], lq[:, 1, width:2 * width], tmp[:, 0:width], lq[:, 0, 0:width])[k - 4]
                lo = width if half == 2 else 0
                return (tmp[:, lo:lo + width], lq[:, 0, lo:lo + width])[k % 2]
            if what == "x1":
                return late[:, 0, :] if half == 1 and k % 2 else late[:, 2, :]
            return tmp[:, :]

        def sum_at(what, half):
            if what == "x":
                return lq[:, 2 + half, :]
            if what == "f":
                return (sum_mix[:, :], lq[:, 2, 0:T // 2], lq[:, 3, 0:T // 2])[half]
            return late[:, 3, :] if what == "x1" else sum_mix[:, :]

        def v_at(h):
            return lq[:, 0, :] if h == 0 else tmp[:, :]

        def x1_back_at(t):
            return late[:, t, :] if t < 4 else raw[:, (t - 4) // 2, T * (t % 2):T * (t % 2) + T]

        small_in, const_in = sem("small_in"), sem("const_in")
        onehot_in = sem("onehot_in")
        x_in = [sem(f"x_in{i}") for i in range(4 * HALVES)]
        raw_in = [sem(f"raw_in{i}") for i in range(RAW)]
        x_again = [sem(f"x_again{i}") for i in range(2)]
        spilled = [sem(f"spilled{h}") for h in range(HALVES)]
        x1_back = [sem(f"x1_back{i}") for i in range(KD)]
        band_out = sem("band_out")
        bias_in = sem("bias_in")
        stored = sem("stored")
        masked_row = sem("masked_row")
        zeros_ready = sem("zeros_ready")
        w_hi, w_lo = sem("w_hi"), sem("w_lo")
        xg_hi, xg_lo = sem("xg_hi"), sem("xg_lo")
        squared, summed, x_summed = sem("squared"), sem("summed"), sem("x_summed")
        item_full, item_evac = sem("item_full"), sem("item_evac")
        root_ready = sem("root_ready")
        split_hi, split_lo = sem("split_hi"), sem("split_lo")
        window_step, pool_step = sem("window_step"), sem("pool_step")
        scores_full, logits_ready, negmax_ready = sem("scores_full"), sem("logits_ready"), sem("negmax_ready")
        exp_ready, denom_step, probs_ready = sem("exp_ready"), sem("denom_step"), sem("probs_ready")
        pt_full, pt_hi, pt_lo = sem("pt_full"), sem("pt_hi"), sem("pt_lo")
        heads_full, heads_hi, heads_lo = sem("heads_full"), sem("heads_hi"), sem("heads_lo")
        x1_step, x1_ready, x1_hi, x1_lo = sem("x1_step"), sem("x1_ready"), sem("x1_hi"), sem("x1_lo")
        gate_full, gate_evac, silu_ready, silu_scaled = (
            sem("gate_full"), sem("gate_evac"), sem("silu_ready"), sem("silu_scaled"))
        up_full, up_evac, hid_hi, hid_lo = sem("up_full"), sem("up_evac"), sem("hid_hi"), sem("hid_lo")
        down_full, down_evac = sem("down_full"), sem("down_evac")
        f_scaled, f_scaled_dve, final_ready = sem("f_scaled"), sem("f_scaled_dve"), sem("final_ready")
        tables_ready = sem("tables_ready")

        PER_GROUP = 3 * FF_PER_GROUP

        def ring_slot(n):
            return n % RING

        def gate_up_slot(s):
            return (N_RING + s) % RING if s < RING else 3

        def weight_cols(n):
            return P if WEIGHTS[n][0] == "mix" else 1024

        def ring_source(n):
            kind, half, which = WEIGHTS[n]
            if kind == "mix":
                return w_pool[which]
            if kind == "out":
                return w_out_t[which]
            order = ("u0", "u1", "u2", "u3", "q0", "q1", "q2", "q3", "k", "v")
            return w_in_t[order.index(which)]

        def window_sums(eng, nc_eng, half, g):
            src = u_buf
            for i in range(g + 1):
                lo, shift, dst = 2 ** (i + 1) - 1, 2 ** i, win[i % 2]
                done = WINDOW_STEPS[(half, g)] - (g + 1) + i
                if done > 0:
                    eng.wait_ge(window_step, done)
                nc_eng.tensor_tensor(dst[:, lo:], src[:, lo:], src[:, lo - shift:HIST + T - shift],
                                     ALU.add).then_inc(window_step, 1)
                src = dst

        block = ctx.enter_context(nc.Block())

        @block.sync
        def _(sp):
            def load_raw(n_parity, count, src, cols):
                sp.wait_ge(w_lo, count - RAW + 1)
                sp.dma_start(raw[:, n_parity, 0:cols], src).then_inc(raw_in[n_parity], 16)

            sp.dma_start(raw[:, 0, :], ring_source(0)).then_inc(raw_in[0], 16)

            def load_x(h):
                for c in range(4):
                    if (h, c) == (0, 1):
                        sp.dma_start(sm[:, :], small).then_inc(small_in, 16)
                    sp.dma_start(big[:, h, 2 * c:2 * c + 2, :], x_t[h, :, 2 * c:2 * c + 2, :]).then_inc(x_in[4 * h + c], 16)

            load_x(0)
            sp.dma_start(raw[:, 1, :], ring_source(1)).then_inc(raw_in[1], 16)
            for n in range(RAW, N_RING):
                load_raw(n % RAW, n, ring_source(n), weight_cols(n))
                if n == 2:
                    sp.dma_start(cst[:, :], consts).then_inc(const_in, 16)
                    sp.dma_start(rel_sb[0:N_BUCKETS, :], rel).then_inc(onehot_in, 16)
                    sp.dma_start(sum_mix[0:N_BUCKETS + 1, 0:BAND], onehot).then_inc(onehot_in, 16)
                if n == 3:
                    load_x(1)

            with sp.Fori(0, GROUPS) as g:
                for s in range(2 * FF_PER_GROUP):
                    w = w_up_t if s % 2 else w_gate_t
                    src = w[bass.ds(g * FF_PER_GROUP + s // 2, 1)].rearrange("a p n -> p (a n)")
                    load_raw(s % RAW, N_RING + PER_GROUP * g + s, src, 1024)
                for c in range(FF_PER_GROUP):
                    src = w_down[bass.ds(g * FF_PER_GROUP + c, 1)].rearrange("a p n -> p (a n)")
                    load_raw(c % RAW, N_RING + PER_GROUP * g + 4 + c, src, 1024)

            sp.wait_ge(item_evac, EVAC[("norm", "x1", 1)])
            for h in range(HALVES):
                sp.wait_ge(spilled[h], 16 * KD)
            for t in range(KD):
                if t == 4:
                    sp.wait_ge(w_lo, N_RING + PER_GROUP * GROUPS)
                sp.dma_start(x1_back_at(t), x1_spill[0, :, t, :]).then_inc(x1_back[t], 16)
            for z in range(3 * KD):
                h, cols = PARTS[z // KD]
                t = z % KD
                sp.wait_ge(final_ready, z + 1)
                sp.dma_start(out_t[h, :, t, cols], big[:, h, t, cols]).then_inc(stored, 16)
                if h == 0:
                    sp.dma_start(x1_back_at(t), x1_spill[1, :, t, :]).then_inc(x1_back[t], 16)
            sp.wait_ge(stored, 16 * 3 * KD)

        @block.gpsimd
        def _(pool):
            def weights_lo(dst_hi, dst_lo, parity, n, cols=1024):
                pool.wait_ge(w_hi, n + 1)
                nc.gpsimd.tensor_tensor(dst_lo[:, 0:cols], raw[:, parity, 0:cols], dst_hi[:, 0:cols].bitcast(F32),
                                        ALU.subtract).then_inc(w_lo, 1)

            def add_square(s):
                if s[2] == 0 or (s[:2] == ("f", 2) and s[2] in LAST_SUMMED_BY_PE):
                    return
                pool.wait_ge(squared, SQUARE_NO[s])
                if ADD_NO[s] > 1:
                    pool.wait_ge(summed, ADD_NO[s] - 1)
                acc = sum_at(s[0], s[1])
                nc.gpsimd.tensor_tensor(acc, acc, square_at(s), ALU.add).then_inc(summed, 1)

            for e in TIMELINE:
                if e[0] == "weights":
                    n = e[1]
                    if n in LO_BY_DVE:
                        continue
                    if n - 1 in LO_BY_DVE:
                        pool.wait_ge(w_lo, n)
                    if n < N_RING:
                        s = ring_slot(n)
                        weights_lo(slots[:, s, HI, :], slots[:, s, LO, :], n % RAW, n, weight_cols(n))
                    else:
                        s = gate_up_slot(n - N_RING)
                        weights_lo(slots[:, s, HI, :], slots[:, s, LO, :], n % RAW, n)
                elif e[0] == "square":
                    add_square(e[1:])
                elif e[0] == "residual":
                    add_square(("x1", e[1], e[2]))
                elif e[0] == "evac" and e[1][0] == "proj" and e[1][1:] not in WINDOWS_BY_DVE and e[1][2][0] == "u":
                    pool.wait_ge(item_evac, EVAC[e[1]])
                    window_sums(pool, nc.gpsimd, e[1][1], int(e[1][2][1]))

            def down_weights(g):
                for c in range(FF_PER_GROUP):
                    weights_lo(wd[:, c, HI, :], wd[:, c, LO, :], c % RAW, N_RING + PER_GROUP * g + 4 + c)

            def gate_up_weights(g):
                for s in range(2 * FF_PER_GROUP):
                    at = gate_up_slot(s)
                    weights_lo(slots[:, at, HI, :], slots[:, at, LO, :], s % RAW, N_RING + PER_GROUP * g + s)

            pool.wait_ge(item_evac, EVAC[("norm", "mix", 1)])
            for t in range(KD):
                at = big[:, 1, t, :]
                nc.gpsimd.tensor_tensor(at, at, rms[:, 1, :], ALU.mult).then_inc(x1_step, 1)
            down_weights(0)
            for t in range(KD):
                add_square(("x1", 1, t))
            gate_up_weights(1)
            with pool.Fori(1, GROUPS - 1) as g:
                down_weights(g)
                gate_up_weights(g + 1)
            down_weights(GROUPS - 1)

            def scale_f(part):
                h, cols = PARTS[part]
                pool.wait_ge(item_evac, EVAC[("norm", "f", part)])
                for t in range(KD):
                    if t not in SCALED_BY_DVE[part]:
                        at = big[:, h, t, cols]
                        nc.gpsimd.tensor_tensor(at, at, rms[:, h, cols], ALU.mult).then_inc(f_scaled, 1)

            for t in range(KD):
                add_square(("f", 0, t))
            scale_f(0)
            for part in (1, 2):
                for t in range(KD):
                    add_square(("f", part, t))
            scale_f(1)
            scale_f(2)

        @block.scalar
        def _(act):
            def weights_hi(dst, parity, n, cols=1024):
                act.wait_ge(raw_in[parity], 16 * (n // RAW + 1) if isinstance(n, int) else n)
                nc.scalar.copy(dst[:, 0:cols], raw[:, parity, 0:cols]).then_inc(w_hi, 1)

            def square(s, src):
                no = SQUARES.index(s)
                if s[2] == 0:
                    if s[:2] in (("mix", 1), ("x1", 1)):
                        last = ("norm", s[0], 0)
                        act.wait_ge(item_full, FULL[last])
                    elif s[:2] == ("f", 0):
                        act.wait_ge(item_full, FULL[("norm", "mix", 1)])
                elif s[0] == "x":
                    if s[2] > 2:
                        act.wait_ge(x_summed, (KD - 1) * s[1] + s[2] - 2)
                else:
                    same = [r for r in SQUARES[:no] if r[2] > 0 and square_place(r) == square_place(s)]
                    if s[:2] == ("f", 2) and s[2] in LAST_SUMMED_BY_PE:
                        act.wait_ge(summed, ADD_NO[("f", 1, KD - 1)])
                    elif same:
                        act.wait_ge(summed, ADD_NO[same[-1]])
                nc.scalar.activation(square_at(s), src, ACT.Square).then_inc(squared, 1)

            def square_place(r):
                what, part, k = r
                return {"x": ("x", k % 2), "x1": ("x1", part * k % 2), "mix": ("tmp", False),
                        "f": (("tmp", "lq")[k % 2], part == 2)}[what]

            def norm_root(item):
                act.wait_ge(item_full, FULL[item])
                h, cols = PARTS[item[2]] if item[1] == "f" else (item[2], slice(0, T))
                nc.scalar.activation(rms[:, h, cols], ps[:, BANK[item], 0:cols.stop - cols.start], ACT.Sqrt,
                                     bias=eps_col, scale=1.0 / D).then_inc(root_ready, 1)

            def residual_hi(h, t):
                z = KD * h + t
                act.wait_ge(x1_ready, z + 1)
                if h == 1 and t + 2 < KD:
                    load_x(h, t + 2)
                nc.scalar.activation(mov[:, HI, h, t, :], big[:, h, t, :], ACT.Copy,
                                     scale=sm[:, G_PRE_FFN + t:G_PRE_FFN + t + 1]).then_inc(x1_hi, 1)
                if h == 0 and t + 2 < KD:
                    load_x(h, t + 2)
                if h == 0:
                    square(("x1", h, t), big[:, h, t, :])
                act.dma_start(x1_spill[h, :, t, :], big[:, h, t, :]).then_inc(spilled[h], 16)

            def load_x(h, t):
                z = KD * h + t
                act.dma_start(late[:, z % 2, :], x_t[h, :, t, :]).then_inc(x_again[z % 2], 16)

            def load_table(func, src):
                nc.scalar.activation(scratch, src, func)

            scratch = stat[:, 0, 6, 0:1]
            eps_col = cst[:, N_CONST - 1:N_CONST]
            act.wait_ge(tables_ready, 1)
            load_table(ACT.Copy, stat[:, 1, 6, 0:1])
            for e in TIMELINE:
                kind = e[0]
                if kind == "weights":
                    n = e[1]
                    if n < N_RING:
                        if n >= RING:
                            act.wait_ge(item_full, FULL[WEIGHTS[n - RING]])
                        if n == 3:
                            act.wait_ge(const_in, 16)
                            load_table(ACT.Sqrt, eps_col)
                        weights_hi(slots[:, ring_slot(n), HI, :], n % RAW, n, weight_cols(n))
                    else:
                        s = n - N_RING
                        if s < RING:
                            act.wait_ge(item_full, FULL[WEIGHTS[N_RING + s - RING]])
                        else:
                            act.wait_ge(heads_full, UNITS)
                        weights_hi(slots[:, gate_up_slot(s), HI, :], n % RAW, n)
                elif kind == "xsplit":
                    h = e[1]
                    if h == 0:
                        act.wait_ge(small_in, 16)
                    for k in range(KD):
                        act.wait_ge(x_in[4 * h + k // 2], 16)
                        nc.scalar.activation(mov[:, HI, h, k, :], big[:, h, k, :], ACT.Copy,
                                             scale=sm[:, G_PRE_MIX + k:G_PRE_MIX + k + 1]).then_inc(xg_hi, 1)
                elif kind == "xsquares":
                    if e[1] == 1:
                        act.wait_ge(item_full, FULL[("vtr", 0)])
                    for k in e[2]:
                        square(("x", e[1], k), big[:, e[1], k, :])
                elif kind == "square":
                    what, h, t = e[1:]
                    act.wait_ge(item_evac, EVAC[("out", h, t)])
                    square((what, h, t), big[:, h, t, :])
                elif kind == "bias_read":
                    act.wait_ge(band_out, 16)
                    rows = bass.AP(tensor=band_rows.tensor, offset=0, ap=[[1, P], [BAND, N_HEADS], [1, 256]])
                    act.dma_start(bias8[:, :].rearrange("p (h k) -> p h k", h=N_HEADS), rows).then_inc(bias_in, 16)
                elif kind == "pool_split":
                    _, h, g = e
                    if h == 1:
                        act.wait_ge(item_evac, EVAC[("proj", 1, "q3")])
                    else:
                        act.wait_ge(item_evac, EVAC[("proj", 0, "q3")])
                    act.wait_ge(pool_step, POOL_STEPS[(h, g)])
                    nc.scalar.copy(mov[:, HI, h, g, :], pooled[:, g, :]).then_inc(split_hi, 1)
                elif kind == "exp":
                    u = e[1]
                    b = u % 2
                    act.wait_ge(negmax_ready, u + 1)
                    nc.scalar.activation(stat[:, b, 3, :], stat[:, b, 2, :], ACT.Exp)
                    k0 = 256 - BLOCK * len(key_blocks(u))
                    for i in range(4):
                        at = lbuf[:, b, 256 * i + k0:256 * i + 256]
                        last = nc.scalar.activation(at, at, ACT.Exp, bias=stat[:, b, 1, i:i + 1],
                                                    accum_out=stat[:, b, 4, i:i + 1])
                    last.then_inc(exp_ready, 1)
                elif kind == "heads_out":
                    u = e[1]
                    h, jp, blk = unit_place(u)
                    act.wait_ge(heads_full, u + 1)
                    dst = mov[:, HI, h, 4 + 2 * jp:6 + 2 * jp, BLOCK * (blk % 4):BLOCK * (blk % 4 + 1)]
                    src = ps[:, 2 * (u % 2), 0:256].rearrange("p (j t) -> p j t", j=2)
                    nc.scalar.copy(dst, src).then_inc(heads_hi, 1)
                elif kind == "split" and e[2] != "k":
                    _, h, name = e
                    act.wait_ge(item_evac, EVAC[("proj", h, name)])
                    for v in range(N_KV):
                        rows = slice(64 * v, 64 * v + 64)
                        last = nc.scalar.copy(q[rows, int(name[1]), v, :], tmp[rows, :])
                    last.then_inc(split_hi, 1)
                elif kind == "split":
                    h = e[1]
                    act.wait_ge(item_evac, EVAC[("proj", h, "k")])
                    for v in range(N_KV):
                        for place in range(2):
                            last = nc.scalar.copy(kk[64 * place:64 * place + 64, HI, v, T * h:T * h + T],
                                                  tmp[64 * v:64 * v + 64, :])
                    last.then_inc(split_hi, 1)
                elif kind == "probs_split":
                    u = e[1]
                    if u >= 1:
                        act.wait_ge(heads_full, u)
                    for kb in key_blocks(u):
                        act.wait_ge(pt_full, PT_COUNT[u] - 1 + kb)
                        nc.scalar.copy(probs_t[:, HI, 512 * kb:512 * kb + 512], ps[:, 4 + kb, :]).then_inc(pt_hi, 1)
                elif kind == "x_load":
                    act.wait_ge(logits_ready, UNITS)
                    load_x(e[1], e[2])
                elif kind == "residual":
                    residual_hi(e[1], e[2])
                elif kind == "evac":
                    item = e[1]
                    if item[0] == "norm":
                        if item == ("norm", "x", 0):
                            act.wait_ge(const_in, 16)
                        norm_root(item)
                    elif item[0] == "bias":
                        act.wait_ge(item_evac, EVAC[item])
                        act.dma_start(band_rows, band_sb).then_inc(band_out, 16)
                    elif item[0] == "vtr":
                        act.wait_ge(item_full, FULL[item])
                        h = item[1]
                        dst = vv[:, HI, 4 * h:4 * h + 4, :].rearrange("p b (c d) -> p b c d", d=64)[:, :, 0:3:2, :]
                        src = ps[:, BANK[item], :].rearrange("p (b c d) -> p b c d", b=4, c=2)
                        nc.scalar.copy(dst, src).then_inc(split_hi, 1)
                    elif item[0] == "mix":
                        _, h, g = item
                        act.wait_ge(item_full, FULL[item])
                        nc.scalar.activation(mov[:, HI, h, g, :], ps[:, BANK[item], :], ACT.Copy,
                                             scale=sm[:, POOL_SCALE + g:POOL_SCALE + g + 1]).then_inc(split_hi, 1)

            def down_weights(g):
                act.wait_ge(down_full, 16 * g)
                for c in range(FF_PER_GROUP):
                    wait_raw(c % RAW, g, 4 + c)
                    nc.scalar.copy(wd[:, c, HI, :], raw[:, c % RAW, :]).then_inc(w_hi, 1)

            def wait_raw(parity, g, c):
                act.wait_ge(raw_in[parity], 16 * ((N_RING + c) // RAW + 1) + 16 * (PER_GROUP // RAW) * g)

            def gate_up_weight(g, s):
                act.wait_ge(up_full if s % 2 else gate_full, 4 * g - 1 + s // 2)
                wait_raw(s % RAW, g, s)
                nc.scalar.copy(slots[:, gate_up_slot(s), HI, :], raw[:, s % RAW, :]).then_inc(w_hi, 1)

            def silu(g, i):
                act.wait_ge(gate_evac, 4 * g + i + 1)
                nc.scalar.activation(lq[:, 1, :], lq[:, 0, :], ACT.Silu).then_inc(silu_ready, 1)

            def hidden_hi(g, i):
                act.wait_ge(up_evac, 4 * g + i + 1)
                nc.scalar.copy(hid[:, i % 2, HI, T * (i // 2):T * (i // 2) + T], lq[:, 2, :]).then_inc(hid_hi, 1)

            def group(g, last=False):
                silu(g, 0)
                hidden_hi(g, 0)
                down_weights(g)
                silu(g, 1)
                hidden_hi(g, 1)
                silu(g, 2)
                if last:
                    for t in range(KD):
                        square_f(0, t)
                    norm_root(("norm", "f", 0))
                    hidden_hi(g, 2)
                    silu(g, 3)
                    hidden_hi(g, 3)
                    return
                gate_up_weight(g + 1, 0)
                hidden_hi(g, 2)
                gate_up_weight(g + 1, 1)
                silu(g, 3)
                gate_up_weight(g + 1, 2)
                hidden_hi(g, 3)
                gate_up_weight(g + 1, 3)

            def first_group():
                norm_root(("norm", "mix", 1))
                silu(0, 0)
                for t in range(KD):
                    residual_hi(1, t)
                    if t == 3:
                        hidden_hi(0, 0)
                    if t in (3, 5):
                        c = t // 5
                        wait_raw(c % RAW, 0, 4 + c)
                        nc.scalar.copy(wd[:, c, HI, :], raw[:, c % RAW, :]).then_inc(w_hi, 1)
                silu(0, 1)
                hidden_hi(0, 1)
                for t in range(KD):
                    square(("x1", 1, t), big[:, 1, t, :])
                norm_root(("norm", "x1", 1))
                silu(0, 2)
                gate_up_weight(1, 0)
                hidden_hi(0, 2)
                gate_up_weight(1, 1)
                silu(0, 3)
                hidden_hi(0, 3)
                gate_up_weight(1, 2)
                gate_up_weight(1, 3)

            def square_f(part, t):
                h, cols = PARTS[part]
                act.wait_ge(down_evac, 16 * (GROUPS - 1) + KD * part + t + 1)
                square(("f", part, t), big[:, h, t, cols])

            act.wait_ge(x1_ready, KD)
            load_x(1, 0)
            load_x(1, 1)
            first_group()
            with act.Fori(1, GROUPS - 1) as g:
                group(g)
            group(GROUPS - 1, last=True)
            load_table(ACT.Sqrt, eps_col)
            act.wait_ge(hid_lo, 4 * GROUPS)
            for t in range(KD):
                square_f(1, t)
            for t in range(KD - 3):
                square_f(2, t)
            norm_root(("norm", "f", 1))
            for t in range(KD - 3, KD):
                square_f(2, t)
            norm_root(("norm", "f", 2))

        @block.vector
        def _(dve):
            steps = {"pool": 0}
            tmp_read = {"lo": 0}

            def norm_reciprocal(item):
                dve.wait_ge(root_ready, NORM_NO[item])
                h, cols = PARTS[item[2]] if item[1] == "f" else (item[2], slice(0, T))
                r = rms[:, h, cols]
                nc.vector.reciprocal(r, r).then_inc(item_evac, 1)

            def x1_scale(t):
                if t == 0:
                    dve.wait_ge(item_evac, EVAC[("norm", "mix", 0)])
                at = big[:, 0, t, :]
                nc.vector.tensor_tensor(at, at, rms[:, 0, :], ALU.mult).then_inc(x1_step, 1)

            def x1_of(h, t):
                z = KD * h + t
                at = big[:, h, t, :]
                dve.wait_ge(x_again[z % 2], 16 * (z // 2 + 1))
                dve.wait_ge(x1_step, z + 1)
                nc.vector.scalar_tensor_tensor(out=at, in0=at, scalar=sm[:, G_POST_MIX + t:G_POST_MIX + t + 1],
                                               in1=late[:, z % 2, :], op0=ALU.mult, op1=ALU.add).then_inc(x1_ready, 1)

            def x1_split(h, t):
                dve.wait_ge(x1_hi, KD * h + t + 1)
                nc.vector.scalar_tensor_tensor(out=mov[:, LO, h, t, :], in0=big[:, h, t, :],
                                               scalar=sm[:, G_PRE_FFN + t:G_PRE_FFN + t + 1],
                                               in1=mov[:, HI, h, t, :].bitcast(F32), op0=ALU.mult,
                                               op1=ALU.subtract).then_inc(x1_lo, 1)

            nc.vector.memset(stat[:, 1, 6, 0:1], 0.0).then_inc(tables_ready, 1)
            nc.vector.memset(rel_sb[N_BUCKETS:N_BUCKETS + 1, :], MASKED).then_inc(masked_row, 1)
            for e in TIMELINE:
                kind = e[0]
                if kind == "weights" and e[1] in LO_BY_DVE:
                    n = e[1]
                    at = slots[:, ring_slot(n) if n < N_RING else gate_up_slot(n - N_RING), :, :]
                    dve.wait_ge(w_hi, n + 1)
                    if n > 0 and n - 1 not in LO_BY_DVE:
                        dve.wait_ge(w_lo, n)
                    nc.vector.tensor_tensor(at[:, LO, :], raw[:, n % RAW, :], at[:, HI, :].bitcast(F32),
                                            ALU.subtract).then_inc(w_lo, 1)
                elif kind == "xsplit":
                    h = e[1]
                    if h == 0:
                        dve.wait_ge(small_in, 16)
                    for k in range(KD):
                        dve.wait_ge(xg_hi, KD * h + k + 1)
                        nc.vector.scalar_tensor_tensor(
                            out=mov[:, LO, h, k, :], in0=big[:, h, k, :], scalar=sm[:, G_PRE_MIX + k:G_PRE_MIX + k + 1],
                            in1=mov[:, HI, h, k, :].bitcast(F32), op0=ALU.mult, op1=ALU.subtract).then_inc(xg_lo, 1)
                elif kind == "xsquares":
                    h = e[1]
                    for k in e[2]:
                        if k > 0:
                            dve.wait_ge(squared, SQUARE_NO[("x", h, k)])
                            if k > 1:
                                dve.wait_ge(x_summed, (KD - 1) * h + k - 1)
                            acc = sum_at("x", h)
                            nc.vector.tensor_tensor(acc, acc, square_at(("x", h, k)), ALU.add).then_inc(x_summed, 1)
                    if h == 0 and KD - 1 in e[2]:
                        nc.vector.memset(vv[:, :, :, 64:128].bitcast(F32), 0.0).then_inc(zeros_ready, 1)
                elif kind == "pool":
                    _, h, g = e
                    w = WINDOWS[g]
                    s = win[g % 2]
                    if (h, f"u{g}") in WINDOWS_BY_DVE:
                        dve.wait_ge(item_evac, EVAC[("proj", h, f"u{g}")])
                        window_sums(dve, nc.vector, h, g)
                    dve.wait_ge(window_step, WINDOW_STEPS[(h, g)])
                    if steps["pool"]:
                        dve.wait_ge(pool_step, steps["pool"])
                    if h == 1:
                        dve.wait_ge(split_lo, LO_NO[("pool_split", 0, g)])
                    nc.vector.scalar_tensor_tensor(out=pooled[:, g, :], in0=s[:, HIST:], scalar=1.0 / w, in1=u_buf[:, HIST:],
                                                   op0=ALU.mult, op1=ALU.subtract).then_inc(pool_step, 1)
                    steps["pool"] += 1
                    if h == 0:
                        if g == 0:
                            dve.wait_ge(const_in, 16)
                        nc.vector.tensor_tensor(fix[:, 0:w - 1], s[:, HIST:HIST + w - 1],
                                                cst[:, INV_COUNT:INV_COUNT + w - 1], ALU.mult).then_inc(pool_step, 1)
                        steps["pool"] += 1
                        dve.wait_ge(pool_step, steps["pool"])
                        nc.vector.tensor_tensor(pooled[:, g, 0:w - 1], fix[:, 0:w - 1], u_buf[:, HIST:HIST + w - 1],
                                                ALU.subtract).then_inc(pool_step, 1)
                        nc.vector.tensor_copy(tails[:, g, :], u_buf[:, T:T + HIST]).then_inc(pool_step, 1)
                        steps["pool"] += 2
                    assert steps["pool"] == POOL_STEPS[(h, g)]
                elif kind == "pool_split":
                    _, h, g = e
                    dve.wait_ge(split_hi, SPLITS[e])
                    nc.vector.tensor_tensor(mov[:, LO, h, g, :], pooled[:, g, :], mov[:, HI, h, g, :].bitcast(F32),
                                            ALU.subtract).then_inc(split_lo, 1)
                elif kind == "logits":
                    u = e[1]
                    _, jp, blk = unit_place(u)
                    b = u % 2
                    k0 = 256 - BLOCK * len(key_blocks(u))
                    from_ = 0 if blk == 0 else k0
                    if u == 0:
                        dve.wait_ge(bias_in, 16)
                    dve.wait_ge(scores_full, u + 1)
                    for i in range(4):
                        head = 4 * jp + i
                        last = nc.vector.tensor_tensor_reduce(
                            out=lbuf[:, b, 256 * i + k0:256 * i + 256],
                            in0=scores_of(u, i // 2)[:, i % 2, from_:from_ + 256 - k0],
                            in1=bias8[:, 256 * head + k0:256 * head + 256], scale=SCALE,
                            scalar=sm[:, SINKS + head:SINKS + head + 1], op0=ALU.add, op1=ALU.max,
                            accum_out=stat[:, b, 0, i:i + 1])
                    last.then_inc(logits_ready, 1)
                    dve.wait_ge(logits_ready, u + 1)
                    sinks = sm[:, SINKS + 4 * jp:SINKS + 4 * jp + 4]
                    nc.vector.tensor_tensor(stat[:, b, 2, :], sinks, stat[:, b, 0, :], ALU.subtract)
                    nc.vector.tensor_scalar(stat[:, b, 1, :], stat[:, b, 0, :], -1.0, None, ALU.mult).then_inc(negmax_ready, 1)
                elif kind == "normalise":
                    u = e[1]
                    b = u % 2
                    k0 = 256 - BLOCK * len(key_blocks(u))
                    dve.wait_ge(exp_ready, u + 1)
                    nc.vector.tensor_tensor(stat[:, b, 5, :], stat[:, b, 3, :], stat[:, b, 4, :],
                                            ALU.add).then_inc(denom_step, 1)
                    dve.wait_ge(denom_step, 2 * u + 1)
                    nc.vector.reciprocal(stat[:, b, 6, :], stat[:, b, 5, :]).then_inc(denom_step, 1)
                    dve.wait_ge(denom_step, 2 * u + 2)
                    for i in range(4):
                        at = lbuf[:, b, 256 * i + k0:256 * i + 256]
                        last = nc.vector.tensor_scalar(at, at, stat[:, b, 6, i:i + 1], None, ALU.mult)
                    last.then_inc(probs_ready, 1)
                elif kind == "heads_out":
                    u = e[1]
                    h, jp, blk = unit_place(u)
                    dve.wait_ge(heads_hi, u + 1)
                    at = (h, slice(4 + 2 * jp, 6 + 2 * jp), slice(BLOCK * (blk % 4), BLOCK * (blk % 4 + 1)))
                    nc.vector.tensor_tensor(mov[:, LO, at[0], at[1], at[2]],
                                            ps[:, 2 * (u % 2), 0:256].rearrange("p (j t) -> p j t", j=2),
                                            mov[:, HI, at[0], at[1], at[2]].bitcast(F32), ALU.subtract).then_inc(heads_lo, 1)
                elif kind == "probs_split":
                    u = e[1]
                    for kb in key_blocks(u):
                        dve.wait_ge(pt_hi, PT_COUNT[u] - 1 + kb)
                        nc.vector.tensor_tensor(probs_t[:, LO, 512 * kb:512 * kb + 512], ps[:, 4 + kb, :],
                                                probs_t[:, HI, 512 * kb:512 * kb + 512].bitcast(F32),
                                                ALU.subtract).then_inc(pt_lo, 1)
                elif kind == "residual":
                    t = e[2]
                    for r in (0, 1) if t == 0 else (t + 1,):
                        if r < KD:
                            x1_scale(r)
                    x1_of(0, t)
                    for r in (t - 1, t) if t == KD - 1 else (t - 1,):
                        if r >= 0:
                            x1_split(0, r)
                elif kind == "split" and e[2] != "k":
                    _, h, name = e
                    dve.wait_ge(split_hi, SPLITS[("proj", h, name)])
                    j = int(name[1])
                    for v in range(N_KV):
                        rows, other = slice(64 * v, 64 * v + 64), slice(64 - 64 * v, 128 - 64 * v)
                        last = nc.vector.tensor_tensor(q[other, j, v, :], tmp[rows, :], q[rows, j, v, :].bitcast(F32),
                                                       ALU.subtract)
                    last.then_inc(split_lo, 1)
                elif kind == "split":
                    h = e[1]
                    dve.wait_ge(split_hi, SPLITS[("proj", h, "k")])
                    for v in range(N_KV):
                        rows, cols = slice(64 * v, 64 * v + 64), slice(T * h, T * h + T)
                        for place in range(2):
                            last = nc.vector.tensor_tensor(kk[64 * place:64 * place + 64, LO, v, cols], tmp[rows, :],
                                                           kk[rows, HI, v, cols].bitcast(F32), ALU.subtract)
                    last.then_inc(split_lo, 1)
                elif kind == "evac":
                    item = e[1]
                    bank = ps[:, BANK[item], :]
                    if item[0] == "norm":
                        norm_reciprocal(item)
                    elif item[0] == "bias":
                        dve.wait_ge(item_full, FULL[item])
                        nc.vector.tensor_scalar(band_sb, bank[0:N_HEADS, 0:BAND], 1.0 / SCALE, None,
                                                ALU.mult).then_inc(item_evac, 1)
                    elif item[0] == "out":
                        dve.wait_ge(item_full, FULL[item])
                        nc.vector.tensor_copy(big[:, item[1], item[2], :], bank).then_inc(item_evac, 1)
                    elif item[0] == "mix":
                        _, h, g = item
                        dve.wait_ge(split_hi, SPLITS[item])
                        nc.vector.scalar_tensor_tensor(
                            out=mov[:, LO, h, g, :], in0=bank, scalar=sm[:, POOL_SCALE + g:POOL_SCALE + g + 1],
                            in1=mov[:, HI, h, g, :].bitcast(F32), op0=ALU.mult, op1=ALU.subtract).then_inc(item_evac, 1)
                    elif item[0] == "vtr":
                        h = item[1]
                        dve.wait_ge(split_hi, SPLITS[item])
                        at = [vv[:, s, 4 * h:4 * h + 4, :].rearrange("p b (c d) -> p b c d", d=64)[:, :, 0:3:2, :]
                              for s in (HI, LO)]
                        nc.vector.tensor_tensor(at[1], bank.rearrange("p (b c d) -> p b c d", b=4, c=2),
                                                at[0].bitcast(F32), ALU.subtract).then_inc(item_evac, 1)
                    elif item[0] == "proj":
                        h, name = item[1:]
                        dve.wait_ge(item_full, FULL[item])
                        dve.wait_ge(item_evac, EVAC[("norm", "x", h)])
                        if name[0] == "u":
                            g = int(name[1])
                            if (h, g) == (0, 0):
                                dve.wait_ge(squared, SQUARE_NO[("x", 1, KD - 1)])
                                dve.wait_ge(xg_lo, HALVES * KD)
                            if steps["pool"]:
                                dve.wait_ge(pool_step, steps["pool"])
                            if h == 0:
                                if g == 0:
                                    nc.vector.memset(u_buf[:, 0:HIST], 0.0)
                            else:
                                nc.vector.tensor_copy(u_buf[:, 0:HIST], tails[:, g, :])
                            nc.vector.tensor_tensor(u_buf[:, HIST:], bank, rms[:, h, :], ALU.mult).then_inc(item_evac, 1)
                        else:
                            if tmp_read["lo"] and item != ("proj", 0, "v"):
                                dve.wait_ge(split_lo, tmp_read["lo"])
                            dst, src, r = v_at(h) if name == "v" else tmp[:, :], bank, rms[:, h, :]
                            if name[0] == "q":
                                dst = dst.rearrange("p (b t) -> p b t", b=4)[:, :, ::-1]
                                src, r = (a.rearrange("p (b t) -> p b t", b=4) for a in (src, r))
                            nc.vector.tensor_tensor(dst, src, r, ALU.mult).then_inc(item_evac, 1)
                            if name != "v":
                                tmp_read["lo"] = LO_NO[item]

            def gate_out(g, i):
                dve.wait_ge(gate_full, 4 * g + i + 1)
                nc.vector.tensor_tensor(lq[:, 0, :], ps[:, 2 * (i % 2), :], rms[:, i // 2, :], ALU.mult).then_inc(gate_evac, 1)
                dve.wait_ge(silu_ready, 4 * g + i + 1)
                nc.vector.tensor_tensor(lq[:, 3, :], lq[:, 1, :], rms[:, i // 2, :], ALU.mult).then_inc(silu_scaled, 1)

            def up_out(g, i):
                dve.wait_ge(up_full, 4 * g + i + 1)
                dve.wait_ge(silu_scaled, 4 * g + i + 1)
                if not (isinstance(g, int) and g == 0 and i == 0):
                    dve.wait_ge(hid_lo, 4 * g + i)
                nc.vector.tensor_tensor(lq[:, 2, :], ps[:, 2 * (i % 2) + 1, :], lq[:, 3, :], ALU.mult).then_inc(up_evac, 1)
                dve.wait_ge(hid_hi, 4 * g + i + 1)
                cols = slice(T * (i // 2), T * (i // 2) + T)
                nc.vector.tensor_tensor(hid[:, i % 2, LO, cols], lq[:, 2, :], hid[:, i % 2, HI, cols].bitcast(F32),
                                        ALU.subtract).then_inc(hid_lo, 1)

            def add_down(g, e, first=False, last=False):
                h, cols = PARTS[e // KD] if last else (e // KD, slice(0, T))
                t = e % KD
                if first and t == 0:
                    dve.wait_ge(spilled[h], 16 * KD)
                dve.wait_ge(down_full, 16 * g + e + 1)
                at, bank = big[:, h, t, cols], ps[:, 4 + e % 4, 0:cols.stop - cols.start]
                if first:
                    nc.vector.tensor_copy(at, bank).then_inc(down_evac, 1)
                else:
                    nc.vector.tensor_tensor(at, at, bank, ALU.add).then_inc(down_evac, 1)

            def scale_f(part, t):
                h, cols = PARTS[part]
                at = big[:, h, t, cols]
                dve.wait_ge(item_evac, EVAC[("norm", "f", part)])
                nc.vector.tensor_tensor(at, at, rms[:, h, cols], ALU.mult).then_inc(f_scaled_dve, 1)

            def final(part, t):
                h, cols = PARTS[part]
                at = big[:, h, t, cols]
                if t in SCALED_BY_DVE[part]:
                    before = sum(len(d) for d in SCALED_BY_DVE[:part])
                    dve.wait_ge(f_scaled_dve, before + SCALED_BY_DVE[part].index(t) + 1)
                else:
                    dve.wait_ge(f_scaled, scaled_by_pool(part, t))
                dve.wait_ge(x1_back[t], 16 * (h + 1))
                nc.vector.scalar_tensor_tensor(out=at, in0=at, scalar=sm[:, G_POST_FFN + t:G_POST_FFN + t + 1],
                                               in1=x1_back_at(t)[:, cols], op0=ALU.mult,
                                               op1=ALU.add).then_inc(final_ready, 1)

            norm_reciprocal(("norm", "mix", 1))
            dve.wait_ge(item_evac, EVAC[("norm", "x1", 0)])
            gate_out(0, 0)
            x1_of(1, 0)
            for t in range(KD):
                if t + 1 < KD:
                    x1_of(1, t + 1)
                x1_split(1, t)
                if t == KD // 2 - 1:
                    up_out(0, 0)
            gate_out(0, 1)
            up_out(0, 1)
            for e in range(KD):
                add_down(0, e, first=True)
            norm_reciprocal(("norm", "x1", 1))
            dve.wait_ge(item_evac, EVAC[("norm", "x1", 1)])
            for i in (2, 3):
                gate_out(0, i)
                up_out(0, i)
            for e in range(KD, 2 * KD):
                add_down(0, e, first=True)
            with dve.Fori(1, GROUPS - 1) as g:
                for i in range(4):
                    gate_out(g, i)
                    up_out(g, i)
                for e in range(16):
                    add_down(g, e)
            g = GROUPS - 1
            gate_out(g, 0)
            up_out(g, 0)
            gate_out(g, 1)
            up_out(g, 1)
            gate_out(g, 2)
            for e in range(KD):
                add_down(g, e, last=True)
            norm_reciprocal(("norm", "f", 0))
            up_out(g, 2)
            final(0, 0)
            gate_out(g, 3)
            for t in range(1, 5):
                final(0, t)
            up_out(g, 3)
            for e in range(KD, 3 * KD):
                add_down(g, e, last=True)
                if e in (KD + 2, KD + 5, KD + 8):
                    final(0, 5 + (e - KD) // 3)
            norm_reciprocal(("norm", "f", 1))
            for t in SCALED_BY_DVE[1]:
                scale_f(1, t)
            norm_reciprocal(("norm", "f", 2))
            for t in range(KD):
                final(1, t)
            for t in SCALED_BY_DVE[2]:
                scale_f(2, t)
            for t in range(KD):
                final(2, t)

        @block.tensor
        def _(pe):
            def product(out, w, x, start, stop):
                nc.tensor.matmul(out, w[HI], x[HI], start=start, stop=False)
                nc.tensor.matmul(out, w[HI], x[LO], start=False, stop=False)
                return nc.tensor.matmul(out, w[LO], x[HI], start=False, stop=stop)

            def weight(s, k):
                return [slots[:, s, part, P * k:P * k + P] for part in (HI, LO)]

            def moving(h, k):
                return [mov[:, part, h, k, :] for part in (HI, LO)]

            def norm_sum(item):
                what, part = item[1:]
                if what == "x":
                    pe.wait_ge(x_summed, (KD - 1) * (part + 1))
                else:
                    pe.wait_ge(summed, ADD_NO[(what, part, KD - 1)])
                bank_free(item)
                for t in LAST_SUMMED_BY_PE if (what, part) == ("f", 2) else ():
                    pe.wait_ge(squared, SQUARE_NO[("f", 2, t)])
                    at = square_at(("f", 2, t))
                    nc.tensor.matmul(ps[:, BANK[item], 0:at.shape[1]], ones, at, start=t == LAST_SUMMED_BY_PE[0], stop=False)
                acc = sum_at(what, part)
                nc.tensor.matmul(ps[:, BANK[item], 0:acc.shape[1]], ones, acc, start=(what, part) != ("f", 2),
                                 stop=True).then_inc(item_full, 1)

            def bank_free(item):
                before = BANK_BEFORE[item]
                if before is not None and before[0] == "norm":
                    pe.wait_ge(root_ready, NORM_NO[before])
                elif before is not None:
                    pe.wait_ge(item_evac, EVAC[before])

            def values(u):
                h, jp, blk = unit_place(u)
                pe.wait_ge(pt_lo, PT_COUNT[u])
                pe.wait_ge(item_evac, EVAC[("vtr", h)])
                out = ps[:, 2 * (u % 2), 0:256]
                kbs = key_blocks(u)
                for kb in kbs:
                    for v in range(N_KV):
                        last = product(out, [vv[:, p_, blk - 1 + kb, 64 * v:64 * v + P] for p_ in (HI, LO)],
                                       [probs_t[:, p_, 512 * kb + 256 * v:512 * kb + 256 * v + 256] for p_ in (HI, LO)],
                                       (kb, v) == (kbs[0], 0), (kb, v) == (1, 1))
                last.then_inc(heads_full, 1)

            n = 0
            for entry in PE_ORDER:
                item = entry[:3]
                kind = item[0]
                if kind in ("proj", "out", "mix"):
                    pe.wait_ge(w_lo, n + 1)
                    bank_free(item)
                    out, slot = ps[:, BANK[item], :], ring_slot(n)
                    if kind == "mix":
                        _, h, g = item
                        pe.wait_ge(split_lo, LO_NO[("pool_split", h, g)])
                        last = product(out, weight(slot, 0), moving(h, g), True, True)
                    else:
                        h = item[1]
                        if kind == "out":
                            pe.wait_ge(item_evac, EVAC[("mix", h, 3)])
                            pe.wait_ge(heads_lo, 8 * (h + 1))
                        for k in range(KD):
                            if kind == "proj":
                                pe.wait_ge(xg_lo, KD * h + k + 1)
                            last = product(out, weight(slot, k), moving(h, k), k == 0, k == KD - 1)
                            if k == 4 and len(entry) > 3:
                                values(entry[4])
                    last.then_inc(item_full, 1)
                    n += 1
                elif kind == "norm":
                    if item == ("norm", "x", 0):
                        pe.wait_ge(const_in, 16)
                    norm_sum(item)
                elif kind == "bias":
                    pe.wait_ge(masked_row, 1)
                    pe.wait_ge(onehot_in, 32)
                    bank_free(item)
                    nc.tensor.matmul(ps[0:N_HEADS, BANK[item], 0:BAND], rel_sb[:, :], sum_mix[0:N_BUCKETS + 1, 0:BAND],
                                     start=True, stop=True).then_inc(item_full, 1)
                elif kind == "vtr":
                    pe.wait_ge(item_evac, EVAC[("proj", item[1], "v")])
                    bank_free(item)
                    for b in range(4):
                        last = nc.tensor.transpose(ps[:, BANK[item], P * b:P * b + P], v_at(item[1])[:, P * b:P * b + P], ident)
                    last.then_inc(item_full, 1)
                elif kind == "scores":
                    u = item[1]
                    h, jp, blk = unit_place(u)
                    if u == 0:
                        pe.wait_ge(zeros_ready, 1)
                        pe.wait_ge(item_evac, max(EVAC[PRE_LAST[b]] for b in range(4)))
                    if u >= 2:
                        pe.wait_ge(heads_lo, u - 1)
                    pe.wait_ge(split_lo, max(LO_NO[("proj", h, n_)] for n_ in ("k", f"q{2 * jp}", f"q{2 * jp + 1}")))
                    keys = slice(BLOCK * max(blk - 1, 0), BLOCK * max(blk - 1, 0) + 256)
                    qs = slice(BLOCK * (blk % 4), BLOCK * (blk % 4 + 1))
                    for jj in range(2):
                        for v in range(N_KV):
                            for part in (HI, LO):
                                last = nc.tensor.matmul(scores_of(u, jj)[:, v, :], q[:, 2 * jp + jj, v, qs],
                                                        kk[:, part, v, keys], start=part == HI, stop=part == LO)
                    last.then_inc(scores_full, 1)
                elif kind == "transpose":
                    u = item[1]
                    pe.wait_ge(probs_ready, u + 1)
                    if u >= 1:
                        pe.wait_ge(pt_lo, PT_COUNT[u - 1])
                    for kb in key_blocks(u):
                        for v in range(N_KV):
                            for jj in range(2):
                                src = lbuf[:, u % 2, 256 * (2 * jj + v) + P * kb:256 * (2 * jj + v) + P * kb + P]
                                last = nc.tensor.transpose(ps[:, 4 + kb, P * (2 * v + jj):P * (2 * v + jj) + P], src, flip)
                        last.then_inc(pt_full, 1)

            def gate(g, i, first=False):
                h, c = i // 2, i % 2
                out = ps[:, 2 * (i % 2), :]
                if not first or i >= 2:
                    pe.wait_ge(gate_evac, 4 * g + i - 1)
                else:
                    pe.wait_ge(heads_lo, UNITS)
                if h == 0:
                    pe.wait_ge(w_lo, N_RING + PER_GROUP * g + 2 * c + 1)
                for k in range(KD):
                    if first and c == 0:
                        pe.wait_ge(x1_lo, KD * h + k + 1)
                    last = product(out, weight(gate_up_slot(2 * c), k), moving(h, k), k == 0, k == KD - 1)
                    if first and i == 0 and k == 5:
                        norm_sum(("norm", "mix", 1))
                last.then_inc(gate_full, 1)

            def up(g, i, first=False, last_group=False):
                h, c = i // 2, i % 2
                out = ps[:, 2 * (i % 2) + 1, :]
                if not first or i >= 2:
                    pe.wait_ge(up_evac, 4 * g + i - 1)
                if h == 0:
                    pe.wait_ge(w_lo, N_RING + PER_GROUP * g + 2 * c + 2)
                for k in range(KD):
                    last = product(out, weight(gate_up_slot(2 * c + 1), k), moving(h, k), k == 0, k == KD - 1)
                    if last_group and i == 2 and k == 5:
                        pe.wait_ge(gate_evac, 4 * g + 3)
                        norm_sum(("norm", "f", 0))
                last.then_inc(up_full, 1)

            def down_wait(g, e, first=False):
                if first and e < 4:
                    if e < 2:
                        pe.wait_ge(pt_lo, PT_COUNT[-1])
                    else:
                        pe.wait_ge(item_evac, EVAC[("norm", "mix", 1)])
                else:
                    pe.wait_ge(down_evac, 16 * g + e - 3)
                    if first and e == KD:
                        pe.wait_ge(item_evac, EVAC[("norm", "x1", 1)])
                if e == 0:
                    pe.wait_ge(w_lo, N_RING + PER_GROUP * g + 6)

            def down_product(e, c, last_group=False):
                h, cols = PARTS[e // KD] if last_group else (e // KD, slice(0, T))
                t = e % KD
                return product(ps[:, 4 + e % 4, 0:cols.stop - cols.start],
                               [wd[:, c, p_, P * t:P * t + P] for p_ in (HI, LO)],
                               [hid[:, c, p_, T * h + cols.start:T * h + cols.stop] for p_ in (HI, LO)],
                               c == 0, c == FF_PER_GROUP - 1)

            def down(g, e, first=False, last_group=False):
                down_wait(g, e, first)
                if e % KD == 0:
                    pe.wait_ge(hid_lo, 4 * g + 2 * min(e // KD, 1) + 2)
                for c in range(FF_PER_GROUP):
                    last = down_product(e, c, last_group)
                last.then_inc(down_full, 1)

            def down_first_four(g, last_group=False):
                pe.wait_ge(hid_lo, 4 * g + 3)
                for e in range(KD, KD + 4):
                    down_wait(g, e, first=g == 0)
                    down_product(e, 0, last_group)
                pe.wait_ge(hid_lo, 4 * g + 4)
                for e in range(KD, KD + 4):
                    down_product(e, 1, last_group).then_inc(down_full, 1)

            for i in range(3):
                gate(0, i, first=True)
                up(0, i, first=True)
            for e in range(KD):
                down(0, e, first=True)
            pe.wait_ge(down_evac, 5)
            norm_sum(("norm", "x1", 1))
            gate(0, 3, first=True)
            up(0, 3, first=True)
            down_first_four(0)
            for e in range(KD + 4, 2 * KD):
                down(0, e, first=True)
            with pe.Fori(1, GROUPS - 1) as g:
                for i in range(4):
                    gate(g, i)
                    up(g, i)
                for e in range(16):
                    down(g, e)
            g = GROUPS - 1
            for i in (0, 1):
                gate(g, i)
                up(g, i)
            gate(g, 2)
            for e in range(KD):
                down(g, e, last_group=True)
            up(g, 2, last_group=True)
            gate(g, 3)
            up(g, 3)
            down_first_four(g, last_group=True)
            for e in range(KD + 4, 3 * KD):
                down(g, e, last_group=True)
                if e == 2 * KD + 4:
                    norm_sum(("norm", "f", 1))
            norm_sum(("norm", "f", 2))


POOL_STEPS, _n = {}, 0
for _e in TIMELINE:
    if _e[0] == "pool":
        _n += 4 if _e[1] == 0 else 1
        POOL_STEPS[_e[1:]] = _n
NORM_NO = {i: n + 1 for n, i in enumerate([i for i in EVACS if i[0] == "norm"])}
LO_NO = {s: n + 1 for n, s in enumerate(s for s in SPLITS if s[0] in ("proj", "pool_split"))}


def _shape_constants():
    consts = np.zeros((P, N_CONST), np.float32)
    consts[:, IDENT:IDENT + P] = np.eye(P, dtype=np.float32)
    consts[:, FLIP:FLIP + P] = np.eye(P, dtype=np.float32)[::-1]
    consts[:, ONES:ONES + P] = 1.0
    consts[:, INV_COUNT:INV_COUNT + HIST - 1] = 1.0 / np.arange(1, HIST, dtype=np.float32)
    consts[:, N_CONST - 1] = EPS
    exact = N_BUCKETS // 2
    dist = np.arange(BLOCK)
    near = np.maximum(dist, 1).astype(np.float32)
    large = exact + (np.log(near / np.float32(exact)) / np.float32(np.log(BLOCK / exact))
                     * np.float32(N_BUCKETS - exact)).astype(np.int32)
    bucket = np.where(dist < exact, dist, np.minimum(large, N_BUCKETS - 1))
    onehot = np.zeros((N_BUCKETS + 1, BAND), np.float32)
    for m in range(BAND):
        d = 2 * BLOCK - 1 - m
        onehot[bucket[d] if 0 <= d < BLOCK else N_BUCKETS, m] = 1.0
    return consts, onehot


def kernel(x, g_pre_mix, w_in, w_pool, pool_scale, rel_bias, sinks, w_out, g_post_mix, g_pre_ffn, w_gate, w_up,
           w_down, g_post_ffn):
    import concourse.bacc as bacc
    from concourse.bass_utils import run_bass_kernel_spmd

    def arr(a):
        return np.asarray(a)

    heads = [h for j in range(4) for h in (j, 4 + j)]
    x_t = np.ascontiguousarray(arr(x)[0].T.reshape(KD, P, HALVES, T).transpose(2, 1, 0, 3))
    cols = [np.arange(512)] + [512 + 64 * h + np.arange(64) for h in heads] + [np.arange(1024, 1280)]
    w_in_p = arr(w_in)[0][:, np.concatenate(cols)]

    def tiles(w):
        k, n = w.shape
        return np.ascontiguousarray(w.reshape(k // P, P, n // P, P).transpose(2, 1, 0, 3).reshape(n // P, P, k))

    rows = np.concatenate([np.arange(512)] + [512 + 64 * h + np.arange(64) for h in heads])
    small = np.concatenate(
        [arr(g)[0].reshape(KD, P).T for g in (g_pre_mix, g_post_mix, g_pre_ffn, g_post_ffn)]
        + [arr(pool_scale)[0].reshape(4, P).T, np.broadcast_to(arr(sinks)[0][heads], (P, N_HEADS))], axis=1)
    consts, onehot = _shape_constants()
    data = {
        "x_t": x_t,
        "small": np.ascontiguousarray(small),
        "consts": consts,
        "rel": np.ascontiguousarray(arr(rel_bias)[:, heads]),
        "onehot": onehot,
        "w_in_t": tiles(w_in_p),
        "w_pool": np.ascontiguousarray(arr(w_pool)[0]),
        "w_out_t": tiles(arr(w_out)[0][rows]),
        "w_gate_t": tiles(arr(w_gate)[0]),
        "w_up_t": tiles(arr(w_up)[0]),
        "w_down": np.ascontiguousarray(arr(w_down)[0].reshape(FF_TILES, P, D)),
    }
    nc = bacc.Bacc("TRN2", target_bir_lowering=False, num_devices=1)
    aps = [nc.dram_tensor(n, a.shape, mybir.dt.from_np(a.dtype), kind="ExternalInput").ap() for n, a in data.items()]
    out = nc.dram_tensor("out_t", [HALVES, P, KD, T], F32, kind="ExternalOutput").ap()
    hybrid_layer(nc, *aps, out)
    r = run_bass_kernel_spmd(nc, [data], core_ids=[0])
    got = np.asarray(r.results[0]["out_t"])
    return np.ascontiguousarray(got.transpose(0, 3, 2, 1).reshape(1, SEQ, D))
```
